# Optimizing a Trainium2 kernel written in Bass

```python
import math
import jax, jax.numpy as jnp
from jax import lax
import numpy as np

D_MODEL = 1024
BATCH = 1
SEQ = 512
DEPTH = 1
DEC_BATCH = 8
DEC_SEQ = 1
PAST_LEN = 1024
PAGE_SIZE = 128

POOL_WIDTH = 256
POOL_WINDOWS = (2, 4, 8, 16)
POOL_GROUPS = len(POOL_WINDOWS)
POOL_GROUP_DIM = POOL_WIDTH // POOL_GROUPS
POOL_BUF = max(POOL_WINDOWS) - 1
ATTN_HEADS = 6
HEAD_DIM = 64
ATTN_WIDTH = ATTN_HEADS * HEAD_DIM
DILATED = ((128, 1), (512, 4), (2048, 16))
ATTN_REACH = max(w for w, _ in DILATED)
ATTN_BLOCK = 128
CONV_WIDTH = D_MODEL - POOL_WIDTH - ATTN_WIDTH
CONV_KERNEL = 31
CONV_BUF = CONV_KERNEL - 1
MIX_WIDTH = POOL_WIDTH + ATTN_WIDTH + CONV_WIDTH
IN_PROJ_WIDTH = POOL_WIDTH + 3 * ATTN_WIDTH + 2 * CONV_WIDTH
N_EXPERTS = 32
TOP_K = 4
D_EXPERT = D_MODEL
SWIGLU_ALPHA = 1.702
SWIGLU_LIMIT = 7.0
MOE_BLOCK = 128
DEEPNORM_ALPHA = (2 * DEPTH) ** 0.25
DEEPNORM_BETA = (8 * DEPTH) ** -0.25
LN_EPS = 1e-5

kernel_name = "hymba_pool_dilated_conformer_moe_step"

def alibi_slopes(n):
    def pow2(k):
        start = 2.0 ** (-8.0 / k)
        return [start ** (i + 1) for i in range(k)]
    if math.log2(n).is_integer():
        s = pow2(n)
    else:
        c = 2 ** math.floor(math.log2(n))
        s = pow2(c) + pow2(2 * c)[0::2][: n - c]
    return jnp.asarray(s, jnp.float32)

def layer_norm(x, g, b):
    xf = x.astype(jnp.float32)
    mu = xf.mean(-1, keepdims=True)
    var = jnp.square(xf - mu).mean(-1, keepdims=True)
    return ((xf - mu) * lax.rsqrt(var + LN_EPS) * g + b).astype(x.dtype)

def pool_mix(u, prefix, pos0, pool_w, pool_scale):
    B, T, _ = u.shape
    ext = jnp.concatenate([prefix, u], axis=1)
    extf = ext.astype(jnp.float32)
    csum = jnp.concatenate([jnp.zeros((B, 1, POOL_WIDTH), jnp.float32), jnp.cumsum(extf, axis=1)], axis=1)
    end = csum[:, POOL_BUF + 1:]
    pos = pos0 + jnp.arange(T)
    diffs = []
    for g, w in enumerate(POOL_WINDOWS):
        sl = slice(g * POOL_GROUP_DIM, (g + 1) * POOL_GROUP_DIM)
        start = csum[:, POOL_BUF + 1 - w: POOL_BUF + 1 - w + T, sl]
        cnt = jnp.minimum(w, pos + 1).astype(jnp.float32)[None, :, None]
        diffs.append((end[..., sl] - start) / cnt - extf[:, POOL_BUF:, sl])
    d = jnp.stack(diffs, axis=2)
    y = jnp.einsum('btgc,gcd->btgd', d, pool_w).reshape(B, T, POOL_WIDTH) * pool_scale
    return y.astype(u.dtype), ext[:, -POOL_BUF:]

def conv_mix(c_in, prefix, conv_w, conv_b, ln_g, ln_b):
    a, gate = jnp.split(c_in, 2, axis=-1)
    u = a * jax.nn.sigmoid(gate)
    ext = jnp.concatenate([prefix, u], axis=1)
    y = lax.conv_general_dilated(ext, conv_w[:, None, :], window_strides=(1,), padding='VALID',
                                 dimension_numbers=('NWC', 'WIO', 'NWC'),
                                 feature_group_count=CONV_WIDTH) + conv_b
    y = jax.nn.silu(layer_norm(y, ln_g, ln_b))
    return y, ext[:, -CONV_BUF:]

def dilated_band_branch(q, k, v, slopes, window, dilation):
    B, S, H, Dh = q.shape
    L = S // dilation
    Lp = -(-L // ATTN_BLOCK) * ATTN_BLOCK
    nb = Lp // ATTN_BLOCK
    n_back = window // dilation

    def to_blocks(x):
        x = x.reshape(B, L, dilation, H, Dh).transpose(0, 2, 1, 3, 4)
        x = jnp.pad(x, ((0, 0), (0, 0), (0, Lp - L), (0, 0), (0, 0)))
        return x.reshape(B, dilation, nb, ATTN_BLOCK, H, Dh)

    def with_prev(xb):
        prev = jnp.pad(xb, ((0, 0), (0, 0), (1, 0), (0, 0), (0, 0), (0, 0)))[:, :, :-1]
        return jnp.concatenate([prev, xb], axis=3)

    qb = to_blocks(q)
    kb = with_prev(to_blocks(k))
    vb = with_prev(to_blocks(v))
    s = jnp.einsum('brnqhd,brnkhd->brnhqk', qb, kb, preferred_element_type=jnp.float32) * (HEAD_DIM ** -0.5)
    qi = jnp.arange(ATTN_BLOCK)[:, None] + ATTN_BLOCK
    ki = jnp.arange(2 * ATTN_BLOCK)[None, :]
    delta = qi - ki
    blk = jnp.arange(nb)[:, None, None]
    valid = (delta >= 0) & (delta <= n_back) & (blk * ATTN_BLOCK + ki - ATTN_BLOCK >= 0)
    bias = -slopes[:, None, None] * (delta * dilation).astype(jnp.float32)[None]
    s = jnp.where(valid[None, None, :, None], s + bias, -jnp.inf)
    m = s.max(-1)
    p = jnp.exp(s - m[..., None])
    l = p.sum(-1)
    acc = jnp.einsum('brnhqk,brnkhd->brnqhd', p, vb.astype(jnp.float32))

    def back(x):
        x = x.reshape((B, dilation, Lp) + x.shape[4:])[:, :, :L]
        x = jnp.swapaxes(x, 1, 2)
        return x.reshape((B, S) + x.shape[3:])

    return back(acc), back(jnp.swapaxes(m, 3, 4)), back(jnp.swapaxes(l, 3, 4))

def dilated_gather_branch(q, k_ext, v_ext, slopes, window, dilation, n_buf, pos0):
    T = q.shape[1]
    n_back = window // dilation
    j = jnp.arange(T)[:, None]
    kk = jnp.arange(n_back + 1)[None, :]
    idx = n_buf + j - kk * dilation
    valid = (idx >= 0) & (pos0 + j - kk * dilation >= 0)
    idx = jnp.maximum(idx, 0)
    kg = k_ext[:, idx]
    vg = v_ext[:, idx]
    s = jnp.einsum('bthd,btkhd->bthk', q, kg, preferred_element_type=jnp.float32) * (HEAD_DIM ** -0.5)
    bias = -slopes[:, None] * (kk * dilation).astype(jnp.float32)
    s = jnp.where(valid[None, :, None, :], s + bias[None, None], -jnp.inf)
    m = s.max(-1)
    p = jnp.exp(s - m[..., None])
    l = p.sum(-1)
    acc = jnp.einsum('bthk,btkhd->bthd', p, vg.astype(jnp.float32))
    return acc, m, l

def merge_dilations(branches):
    acc = jnp.stack([b[0] for b in branches])
    m = jnp.stack([b[1] for b in branches])
    l = jnp.stack([b[2] for b in branches])
    w = jnp.exp(m - m.max(0))
    denom = (w * l).sum(0)
    return (w[..., None] * acc).sum(0) / denom[..., None]

def moe_ffn(h, router_w, router_b, e_w_in, e_b_in, e_w_out, e_b_out):
    B, T, D = h.shape
    xt = h.reshape(-1, D)
    M = xt.shape[0]
    logits = jnp.einsum('md,de->me', xt, router_w, preferred_element_type=jnp.float32) + router_b
    top_v, top_i = lax.top_k(logits, TOP_K)
    gates = jax.nn.softmax(top_v, axis=-1)
    P = M * TOP_K
    e_flat = top_i.reshape(-1)
    t_flat = jnp.repeat(jnp.arange(M, dtype=jnp.int32), TOP_K)
    g_flat = gates.reshape(-1)
    order = jnp.argsort(e_flat)
    es, ts, gs = e_flat[order], t_flat[order], g_flat[order]
    counts = jnp.bincount(e_flat, length=N_EXPERTS)
    starts = jnp.cumsum(counts) - counts
    padded = (counts + MOE_BLOCK - 1) // MOE_BLOCK * MOE_BLOCK
    pad_end = jnp.cumsum(padded)
    pad_start = pad_end - padded
    dest = pad_start[es] + jnp.arange(P) - starts[es]
    n_blocks = -(-P // MOE_BLOCK) + N_EXPERTS
    n_slots = n_blocks * MOE_BLOCK
    slot_tok = jnp.full((n_slots,), M, jnp.int32).at[dest].set(ts)
    slot_gate = jnp.zeros((n_slots,), jnp.float32).at[dest].set(gs)
    block_exp = jnp.minimum(jnp.searchsorted(pad_end, jnp.arange(n_blocks) * MOE_BLOCK, side='right'), N_EXPERTS - 1)
    x_pad = jnp.concatenate([xt, jnp.zeros((1, D), xt.dtype)], axis=0)
    xb = x_pad[slot_tok].reshape(n_blocks, MOE_BLOCK, D)

    def run_block(args):
        xblk, e = args
        hh = xblk @ e_w_in[e] + e_b_in[e]
        gate, up = jnp.split(hh, 2, axis=-1)
        gate = jnp.minimum(gate, SWIGLU_LIMIT)
        up = jnp.clip(up, -SWIGLU_LIMIT, SWIGLU_LIMIT)
        act = gate * jax.nn.sigmoid(SWIGLU_ALPHA * gate) * (up + 1)
        return act @ e_w_out[e] + e_b_out[e]

    yb = lax.map(run_block, (xb, block_exp)).reshape(n_slots, D)
    y = jax.ops.segment_sum(yb.astype(jnp.float32) * slot_gate[:, None], slot_tok, num_segments=M + 1)[:M]
    return y.reshape(B, T, D).astype(h.dtype)

def decoder_layer(x, pool_prefix, conv_prefix, k_prefix, v_prefix, pos0,
                  w_in, pool_w, pool_scale, conv_w, conv_b, conv_ln_g, conv_ln_b, w_o,
                  ln1_g, ln1_b, router_w, router_b, e_w_in, e_b_in, e_w_out, e_b_out,
                  ln2_g, ln2_b, slopes):
    B, T, _ = x.shape
    proj = jnp.einsum('btd,de->bte', x, w_in)
    P, A = POOL_WIDTH, ATTN_WIDTH
    u_pool, q, k, v, c_in = jnp.split(proj, [P, P + A, P + 2 * A, P + 3 * A], axis=-1)
    q = q.reshape(B, T, ATTN_HEADS, HEAD_DIM)
    k = k.reshape(B, T, ATTN_HEADS, HEAD_DIM)
    v = v.reshape(B, T, ATTN_HEADS, HEAD_DIM)
    y_pool, pool_state = pool_mix(u_pool, pool_prefix, pos0, pool_w, pool_scale)
    if k_prefix is None:
        branches = [dilated_band_branch(q, k, v, slopes, w, d) for w, d in DILATED]
    else:
        n_buf = k_prefix.shape[1]
        k_ext = jnp.concatenate([k_prefix, k], axis=1)
        v_ext = jnp.concatenate([v_prefix, v], axis=1)
        branches = [dilated_gather_branch(q, k_ext, v_ext, slopes, w, d, n_buf, pos0) for w, d in DILATED]
    y_attn = merge_dilations(branches).reshape(B, T, ATTN_WIDTH).astype(x.dtype)
    y_conv, conv_state = conv_mix(c_in, conv_prefix, conv_w, conv_b, conv_ln_g, conv_ln_b)
    mix = jnp.concatenate([y_pool, y_attn, y_conv], axis=-1) @ w_o
    x = layer_norm(DEEPNORM_ALPHA * x + mix, ln1_g, ln1_b)
    x = layer_norm(DEEPNORM_ALPHA * x + moe_ffn(x, router_w, router_b, e_w_in, e_b_in, e_w_out, e_b_out), ln2_g, ln2_b)
    return x, pool_state, conv_state, k, v

def setup_inputs(seed: int = 0) -> dict:
    key = jax.random.key(seed)
    ks = jax.random.split(key, 24)
    f32 = jnp.float32
    n_buf = min(ATTN_REACH, PAST_LEN)
    nrm = lambda k, s: jax.random.normal(k, s, f32)
    return {
        "x_prompt": nrm(ks[0], (BATCH, SEQ, D_MODEL)),
        "x_sample": nrm(ks[1], (DEC_BATCH, DEC_SEQ, D_MODEL)),
        "state_pool": nrm(ks[2], (DEPTH, DEC_BATCH, POOL_BUF, POOL_WIDTH)),
        "state_conv": 0.5 * nrm(ks[3], (DEPTH, DEC_BATCH, CONV_BUF, CONV_WIDTH)),
        "cache_attn_k": nrm(ks[4], (DEPTH, DEC_BATCH, n_buf, ATTN_HEADS, HEAD_DIM)),
        "cache_attn_v": nrm(ks[5], (DEPTH, DEC_BATCH, n_buf, ATTN_HEADS, HEAD_DIM)),
        "w_in": nrm(ks[6], (DEPTH, D_MODEL, IN_PROJ_WIDTH)) * D_MODEL ** -0.5,
        "pool_w": nrm(ks[7], (DEPTH, POOL_GROUPS, POOL_GROUP_DIM, POOL_GROUP_DIM)) * POOL_GROUP_DIM ** -0.5,
        "pool_scale": 1.0 + 0.02 * nrm(ks[8], (DEPTH, POOL_WIDTH)),
        "conv_w": nrm(ks[9], (DEPTH, CONV_KERNEL, CONV_WIDTH)) * CONV_KERNEL ** -0.5,
        "conv_b": 0.01 * nrm(ks[10], (DEPTH, CONV_WIDTH)),
        "conv_ln_g": 1.0 + 0.02 * nrm(ks[11], (DEPTH, CONV_WIDTH)),
        "conv_ln_b": 0.01 * nrm(ks[12], (DEPTH, CONV_WIDTH)),
        "w_o": nrm(ks[13], (DEPTH, MIX_WIDTH, D_MODEL)) * MIX_WIDTH ** -0.5 * DEEPNORM_BETA,
        "ln1_g": 1.0 + 0.02 * nrm(ks[14], (DEPTH, D_MODEL)),
        "ln1_b": 0.01 * nrm(ks[15], (DEPTH, D_MODEL)),
        "router_w": nrm(ks[16], (DEPTH, D_MODEL, N_EXPERTS)) * D_MODEL ** -0.5,
        "router_b": 0.01 * nrm(ks[17], (DEPTH, N_EXPERTS)),
        "expert_w_in": nrm(ks[18], (DEPTH, N_EXPERTS, D_MODEL, 2 * D_EXPERT)) * D_MODEL ** -0.5,
        "expert_b_in": 0.01 * nrm(ks[19], (DEPTH, N_EXPERTS, 2 * D_EXPERT)),
        "expert_w_out": nrm(ks[20], (DEPTH, N_EXPERTS, D_EXPERT, D_MODEL)) * D_EXPERT ** -0.5 * DEEPNORM_BETA,
        "expert_b_out": 0.01 * nrm(ks[21], (DEPTH, N_EXPERTS, D_MODEL)),
        "ln2_g": 1.0 + 0.02 * nrm(ks[22], (DEPTH, D_MODEL)),
        "ln2_b": 0.01 * nrm(ks[23], (DEPTH, D_MODEL)),
    }

def reference(x_prompt, x_sample, state_pool, state_conv, cache_attn_k, cache_attn_v,
              w_in, pool_w, pool_scale, conv_w, conv_b, conv_ln_g, conv_ln_b, w_o,
              ln1_g, ln1_b, router_w, router_b, expert_w_in, expert_b_in, expert_w_out,
              expert_b_out, ln2_g, ln2_b):
    slopes = alibi_slopes(ATTN_HEADS)
    y_p, y_s = x_prompt, x_sample
    Bp, Sp, _ = x_prompt.shape
    keep = min(ATTN_REACH, Sp)
    p_pool, p_conv, p_k, p_v = [], [], [], []
    s_pool, s_conv, s_k, s_v = [], [], [], []
    for l in range(DEPTH):
        lw = (w_in[l], pool_w[l], pool_scale[l], conv_w[l], conv_b[l], conv_ln_g[l], conv_ln_b[l], w_o[l],
              ln1_g[l], ln1_b[l], router_w[l], router_b[l], expert_w_in[l], expert_b_in[l],
              expert_w_out[l], expert_b_out[l], ln2_g[l], ln2_b[l], slopes)
        pool0 = jnp.zeros((Bp, POOL_BUF, POOL_WIDTH), x_prompt.dtype)
        conv0 = jnp.zeros((Bp, CONV_BUF, CONV_WIDTH), x_prompt.dtype)
        y_p, ps, cs, kn, vn = decoder_layer(y_p, pool0, conv0, None, None, 0, *lw)
        p_pool.append(ps)
        p_conv.append(cs)
        p_k.append(kn[:, -keep:])
        p_v.append(vn[:, -keep:])
        y_s, ps2, cs2, kn2, vn2 = decoder_layer(y_s, state_pool[l], state_conv[l], cache_attn_k[l],
                                                cache_attn_v[l], PAST_LEN, *lw)
        s_pool.append(ps2)
        s_conv.append(cs2)
        s_k.append(kn2)
        s_v.append(vn2)
    return (y_p, y_s, jnp.stack(p_pool), jnp.stack(p_conv), jnp.stack(p_k), jnp.stack(p_v),
            jnp.stack(s_pool), jnp.stack(s_conv), jnp.stack(s_k), jnp.stack(s_v))


_drawn_inputs = setup_inputs


def setup_inputs(seed=0):
    import zlib

    import numpy as np

    out = dict(_drawn_inputs(seed))
    spreads = {}
    factors = {'pool_scale': 6.835,
     'conv_b': 5.155,
     'conv_ln_g': 6.415,
     'conv_ln_b': 24.825,
     'ln1_b': 3.163,
     'router_b': 4.191,
     'expert_b_in': 8.0,
     'expert_b_out': 8.0,
     'ln2_g': 7.732,
     'ln2_b': 16.273}
    for name, (base, spread) in spreads.items():
        noise = np.random.default_rng([zlib.crc32(name.encode()), seed]).standard_normal(out[name].shape)
        drawn = base * np.exp(spread * noise) if base else spread * noise
        out[name] = __import__('jax').numpy.asarray(drawn.astype(out[name].dtype))
    for name, factor in factors.items():
        out[name] = (out[name] * factor).astype(out[name].dtype)
    return out
```

```python
import math
from contextlib import ExitStack

import numpy as np

import concourse.bass as bass
from concourse import mybir

F32 = mybir.dt.float32
BF16 = mybir.dt.bfloat16
F16 = mybir.dt.float16
I32 = mybir.dt.int32
U32 = mybir.dt.uint32
ALU = mybir.AluOpType
ACT = mybir.ActivationFunctionType
AX = mybir.AxisListType

P = 128
D = 1024
KT = D // P
SEQ = 512
NS = 8
R = SEQ + NS
HALF = R // 2
NT = SEQ // P
POOLW, ATTW, CONVW = 256, 384, 384
NH, HD = 6, 64
PROJ = POOLW + 3 * ATTW + 2 * CONVW
WINDOWS = (2, 4, 8, 16)
PBUF = max(WINDOWS) - 1
TAPS = 31
CBUF = TAPS - 1
PAST = 1024
DILATED = ((128, 1), (512, 4), (2048, 16))
NE, TOPK = 32, 4
FF = 1024
FT = FF // P
ALPHA_N = 2.0 ** 0.25
EPS = 1e-5
SW_ALPHA, SW_LIMIT = 1.702, 7.0
MASKED = -1e30

CAP = 2 * P
NOVER = 8
NJ = NE + NOVER
PAD0 = R
NROW = R + CAP
FEW = P // 2
TWICE = 3 * CAP

def _columns(widths):
    at, out = 0, {}
    for name, w in widths:
        out[name] = (at, at + w)
        at += w
    return out, at

CONST, NCONST = _columns([
    ("ident", P), ("tri", P), ("ones", P), ("mean", P), ("invw", 2), ("cnt", 2 * PBUF), ("wmask", 2 * PBUF),
    ("sel", NS * P), ("spread", NH * NS), ("headof", NH), ("sbias", 2 * P + 1), ("gather", NS),
    ("diag", NH * NS), ("pad", 2), ("part", NT + 1), ("tile0", NT + 1), ("exp", NE), ("jobno", NOVER)])
CHAN, NCHAN = _columns([("taps", 3 * TAPS), ("cb", 3), ("cg", 3), ("cbeta", 3), ("ps", 2)])


def slopes():
    def pow2(k):
        start = 2.0 ** (-8.0 / k)
        return [start ** (i + 1) for i in range(k)]
    c = 2 ** math.floor(math.log2(NH))
    return np.array(pow2(c) + pow2(2 * c)[0::2][:NH - c], np.float32)


def log_count(delta):
    n = sum(((delta >= 0) & (delta <= w) & (delta % d == 0)).astype(np.float64) for w, d in DILATED)
    return np.where(n > 0, np.log(np.maximum(n, 1)), MASKED)


def sample_rows():
    return np.concatenate([np.arange(PAST - P, PAST), np.arange(512, PAST - P, 4), np.arange(0, 512, 16)])


def constants():
    c = np.zeros((P, NCONST), np.float32)

    def put(name, a):
        lo, hi = CONST[name]
        a = np.asarray(a, np.float32)
        c[:a.shape[0], lo:hi] = a.reshape(a.shape[0], hi - lo)
    p = np.arange(P)
    put("ident", np.eye(P))
    put("tri", (p[:, None] < p[None, :]))
    put("ones", np.ones((P, P)))
    put("mean", np.full((P, P), 1.0 / CONVW))
    w = np.array([[WINDOWS[2 * i + (q // HD)] for i in range(2)] for q in range(P)])
    put("invw", 1.0 / w)
    t = np.arange(PBUF)
    put("cnt", 1.0 / np.minimum(w[:, :, None], t + 1))
    put("wmask", t[None, None, :] >= PBUF - (w[:, :, None] - 1))
    put("sel", np.repeat(np.eye(NS)[:, :, None], P, 2))
    b, h = np.divmod(np.arange(NS * NH), NH)
    put("spread", (b[None, :] == np.arange(NS)[:, None]))
    put("headof", (h[:, None] == np.arange(NH)))
    delta = np.append(PAST - sample_rows(), 0)
    put("sbias", log_count(delta) - slopes()[h][:, None] * delta)
    put("gather", b[:, None] == np.arange(NS))
    hb = np.arange(NH * NS)
    put("diag", (h[:, None] == hb // NS) & (b[:, None] == hb % NS))
    put("pad", -(PAD0 + p[:, None] + P * np.arange(2)))
    put("part", np.tile(p[:, None], (1, NT + 1)))
    put("tile0", np.tile(P * np.arange(NT + 1), (P, 1)))
    put("exp", np.tile(np.arange(NE), (P, 1)))
    put("jobno", np.tile(np.arange(NOVER), (P, 1)))
    return c


def slot_ranks():
    few = np.concatenate([np.arange(FEW), np.arange(FEW), np.full(CAP - 2 * FEW, 4 * CAP)])
    return np.tile(np.append(np.arange(TWICE), few).astype(np.float16), (P, 1))


def prompt_bias():
    delta = np.arange(P)[:, None] + (NT - 1) * P - np.arange(SEQ)[None, :]
    b = log_count(delta)[:, None, :] - slopes()[None, :, None] * delta[:, None, :]
    return np.maximum(b, MASKED * 2).astype(np.float32)


STEPS = (["gate0", "a0", "gate1", "a1", "gate2", "a2", "k0", "k1", "k2", "q0", "q1", "q2"]
         + [f"v{i}" for i in range(NT + 1)] + ["pool0", "pool1"] + [f"kt{i}" for i in range(NT)]
         + ["ks", "qs", "states", "mean", "var", "pw0", "pw1"] + [f"qb{b}" for b in range(NS)]
         + ["snew", "st", "pst", "snew2", "sy", "pv0", "pv1", "pv2"]
         + ["wo0", "wo1", "bo0", "wo2", "bo1", "wo3", "bo2", "wo4", "bo3", "bo4"])
STEP = {name: i for i, name in enumerate(STEPS)}


class Chain:

    def __init__(self, eng, sem, base=0):
        self.eng, self.sem, self.base, self.n = eng, sem, base, 0

    def mark(self, ins):
        self.n += 1
        ins.then_inc(self.sem, 1)
        return self.n

    def wait(self, n=None):
        self.eng.wait_ge(self.sem, self.base + (self.n if n is None else n))

    def do(self, ins):
        self.mark(ins)
        self.wait()


def layer(nc, xT, x_prompt, x_sample, pool_prefix, conv_prefix, state_pool, state_conv, cache_k, cache_v,
          w_in, pool_w, chan, w_o, ln1_g, ln1_b, router_w, router_b, e_in, e_bin, e_out, e_bout,
          ln2_g, ln2_b, consts, ranks, pbias,
          y_prompt, y_sample, p_pool, p_conv, p_k, p_v, s_pool, s_conv, s_k, s_v):
    x1_dram = nc.dram_tensor("x1_rows", [R, D], F32).ap()
    acc_dram = nc.dram_tensor("acc_rows", [NROW, D], F32).ap()

    with ExitStack() as outer:
        def keep(name, shape, dt=F32):
            return outer.enter_context(nc.sbuf_tensor(name, shape, dt))

        def sem(name):
            return outer.enter_context(nc.semaphore(name))

        ring = keep("ring", [P, 6, 4096])
        cst = keep("cst", [P, NCONST])
        slot_rank = keep("slot_rank", [P, TWICE + CAP], F16)
        rankm = keep("rankm", [P, NT + 1, NE])
        gates = keep("gates", [P, NT + 1, NE])
        jobs = keep("jobs", [1, 3, NJ + 2], I32)
        njobs = keep("njobs", [1, 1], I32)
        binT = keep("binT", [P, NE, 2 * FT])

        def C(name, rows=P):
            lo, hi = CONST[name]
            return cst[0:rows, lo:hi]

        chunk_in = [sem(f"chunk_in{c}") for c in range(6)]

        def load_chunk(eng, e, c):
            if c < 4:
                for g in range(2):
                    eng.dma_start(ring[:, c].rearrange("p (k a n) -> p k a n", k=KT, a=2)[:, :, g],
                                  e_in[bass.ds(e, 1), :, g * FF + 256 * c:g * FF + 256 * (c + 1)]
                                  .rearrange("o (k p) n -> p (o k) n", p=P)).then_inc(chunk_in[c], 16)
            else:
                eng.dma_start(ring[:, c].rearrange("p (k n) -> p k n", k=FT),
                              e_out[bass.ds(e, 1), :, 512 * (c - 4):512 * (c - 3)]
                              .rearrange("o (k p) n -> p (o k) n", p=P)).then_inc(chunk_in[c], 16)

        first_block(nc, locals())
        moe_block(nc, locals())



def first_block(nc, o):
    xT, x_prompt, x_sample, w_in, w_o, cache_k, cache_v, state_pool, state_conv = (
        o[k] for k in "xT x_prompt x_sample w_in w_o cache_k cache_v state_pool state_conv".split())
    ring, rankm, gates, jobs, njobs, binT, C, sem, load_chunk = (
        o[k] for k in "ring rankm gates jobs njobs binT C sem load_chunk".split())
    x1_dram, acc_dram = o["x1_dram"], o["acc_dram"]

    flat = ring[:, :, :].rearrange("p c n -> p (c n)")
    win = flat[:, 0:KT * PROJ].rearrange("p (k n) -> p k n", k=KT)
    wo = flat[:, 0:KT * D].rearrange("p (k n) -> p k n", k=KT)
    vc0 = KT * D
    vc = flat[:, vc0:vc0 + NS * 2 * ATTW].rearrange("p (b t f) -> p b t f", b=NS, t=2)
    pt0 = vc0 + NS * 2 * ATTW
    pt = flat[:, pt0:pt0 + 2 * NT * SEQ].rearrange("p (u j q) -> p u j q", u=2, j=NT)
    kc0 = 6 * 4096 - NS * 2 * ATTW
    assert pt0 + 2 * NT * SEQ <= kc0 and KT * PROJ <= kc0
    kc = flat[:, kc0:].rearrange("p (b t f) -> p b t f", b=NS, t=2)
    sc = flat[:, kc0:kc0 + 2 * SEQ].rearrange("p (u q) -> p u q", u=2)
    pr = flat[:, kc0 + 2 * SEQ:kc0 + 4 * SEQ].rearrange("p (u q) -> p u q", u=2)
    pb = flat[:, kc0 + 4 * SEQ:kc0 + 10 * SEQ].rearrange("p (h q) -> p h q", h=NH)

    with ExitStack() as ctx:
        def sb(name, shape, dt=F32):
            return ctx.enter_context(nc.sbuf_tensor(name, shape, dt))

        def bsem(name):
            return ctx.enter_context(nc.semaphore(name))

        xt = sb("xt", [P, KT, R])
        late = xt[:, :, :].rearrange("p k r -> p (k r)")
        l1g, l1b = late[:, 0:D], late[:, D:2 * D]
        x1t = late[:, 2 * D:4 * D].rearrange("p (u k r) -> p u k r", u=2, k=KT)
        mix = sb("mix", [P, KT, R])
        scr = mix[:, 2:4, :]
        scr2 = mix[:, 4:6, :]
        prod = mix[:, 2:4, :].rearrange("p a r -> p (a r)")[:, 0:2 * ATTW].rearrange("p (t f) -> p t f", t=2)
        up = sb("up", [P, 2, PBUF + R])
        qT = sb("qT", [P, 3, R])
        kT = sb("kT", [P, 3, R])
        v = sb("v", [P, NT + 1, ATTW])
        conv = sb("conv", [P, 3 * R + 3 * (CBUF + R) + 3 * R])
        sig = conv[:, 0:3 * R].rearrange("p (i r) -> p i r", i=3)
        u = conv[:, 3 * R:6 * R + 3 * CBUF].rearrange("p (i r) -> p i r", i=3)
        cy = conv[:, 6 * R + 3 * CBUF:9 * R + 3 * CBUF].rearrange("p (i r) -> p i r", i=3)
        rst = u[:, 0, 0:R]
        x1 = conv[:, 0:2 * D].rearrange("p (u n) -> p u n", u=2)
        bout = conv[0:NE, 2 * D:3 * D]
        accs = conv[:, 3 * D:4 * D]
        xtok = sb("xtok", [P, 2, D])
        ktok = xtok[:, 0, 0:2 * ATTW].rearrange("p (u f) -> p u f", u=2)
        ksam, qsam = xtok[0:NS, 1, 0:ATTW], xtok[0:NS, 1, ATTW:2 * ATTW]
        chan = sb("chan_sb", [P, NCHAN])
        pw = sb("pw", [P, 2, P])
        ppre = sb("ppre", [P, 2, NS, PBUF])
        cpre = sb("cpre", [P, 3, NS, CBUF])
        rw = sb("rw", [P, KT, NE])
        rb = sb("rb", [1, NE])
        st = sb("st", [NS + CBUF, POOLW + CONVW])
        ssc = sb("ssc", [P, 2, NH * NS])
        s48w = sb("s48", [NH * NS, 5 * NE + 3 * (NJ + 2)])
        s48 = s48w[:, 0:2 * P + 1]
        col48 = sb("col48", [NH * NS, 8])
        ps48 = sb("ps48", [P, 2, NH * NS])
        dg48 = sb("dg48", [NH * NS, NH * NS])
        dnew = sb("dnew", [NS, NH, NS])
        sn = sb("sn", [NS, NH])
        pool8 = sb("pool8", [P, 2, NS])
        conv8 = sb("conv8", [P, 3, NS])
        nsteps = NH * NT
        negm = sb("negm", [P, 4, nsteps])
        bn = sb("bn", [P, 2, 6])
        mv = sb("mv", [P, 4])
        lg = sb("lg", [P, NE])
        top = sb("top", [P, 8])
        topi = sb("topi", [P, 8], U32)
        tf = sb("tf", [P, 16])
        oh4 = sb("oh4", [P, TOPK, NE])
        og4 = sb("og4", [P, TOPK, NE])
        memb = sb("memb", [P, NT + 1, NE])
        gT = sb("gT", [NE, P])
        jr = s48[0:1, 0:5 * NE].rearrange("p (k e) -> p k e", e=NE)
        jv = late[0:1, 2 * D:2 * D + 3 * NOVER * NE].rearrange("p (k v e) -> p k v e", k=3, e=NE)
        jf = s48w[0:1, 5 * NE:5 * NE + 3 * (NJ + 2)].rearrange("p (k j) -> p k j", k=3)
        zero = cpre[:, 0:2].rearrange("p i b t -> p (i b t)")[:, 0:D // 4]

        def chn(name):
            lo, hi = CHAN[name]
            return chan[:, lo:hi]
        taps = chn("taps").rearrange("p (i k) -> p i k", i=3)

        pair = [ctx.enter_context(nc.psum_tensor(f"pair{i}", [P, 2, 512], F32)) for i in range(2)]
        bS = [ctx.enter_context(nc.psum_tensor(f"bS{i}", [P, 512], F32)) for i in range(2)]
        bT = [ctx.enter_context(nc.psum_tensor(f"bT{i}", [P, 512], F32)) for i in range(2)]

        def bank(name):
            return pair[STEP[name] % 2]

        ld = {k: bsem(f"ld_{k}") for k in
              "xt gate0 a0 gate1 a1 gate2 a2 k q v pool cst ranks chan pw ppre cpre rw rb kc vc pb wo l1 xr0 xr1 bout bin"
              .split()}
        pe_step = bsem("pe_step")
        pair_free = [bsem(f"pair_free{i}") for i in range(2)]
        zeroed = bsem("zeroed")
        zero_made = bsem("zero_made")
        copied = bsem("state_copied")
        stored = bsem("stored")
        k_stored = [bsem(f"k_stored{i}") for i in range(2)]
        conv_done = bsem("conv_done")
        centered = bsem("centered")
        squared = bsem("squared")
        z_done = bsem("z_done")
        rst_done = bsem("rst_done")
        var_ready = bsem("ln1_var_ready")
        rstd_ready = bsem("ln1_rstd_ready")
        swish = bsem("swish")
        conv_out = bsem("conv_out")
        pool_d = bsem("pool_d")
        scored = bsem("sample_scored")
        sn_done = bsem("new_scored")
        s_exp = bsem("sample_exp")
        s_neg = bsem("sample_negmax")
        s_prob = bsem("sample_prob")
        qk_done = bsem("qk_done")
        s_max = bsem("row_max")
        exp_done = bsem("exp_done")
        s_recip = bsem("row_recip")
        normed = bsem("normed")
        tr_done = bsem("tr_done")
        pt_done = bsem("pt_done")
        pv_even = bsem("pv_even")
        x_scaled = bsem("x_scaled")
        x1_ready = bsem("x1_ready")
        x1_sent = [bsem(f"x1_sent{i}") for i in range(2)]
        acc_ready = bsem("acc_ready")
        acc_sent = bsem("acc_sent")
        x1T_done = bsem("x1T_done")
        x1T_ready = bsem("x1T_ready")
        lg_done = bsem("lg_done")
        top_neg = bsem("top_neg")
        top_exp = bsem("top_exp")
        g_ready = bsem("gates_ready")
        gT_done = bsem("gT_done")
        gT_ready = bsem("gT_ready")
        m_ready = bsem("members_ready")
        rank_done = bsem("rank_done")
        dve = bsem("dve_chain")
        act = bsem("act_chain")
        pool = bsem("pool_chain")

        def stepped(eng, name):
            eng.wait_ge(pe_step, STEP[name] + 1)

        def freed(name):
            return pair_free[STEP[name] % 2]

        def emptied(eng, name):
            eng.wait_ge(freed(name), STEP[name] // 2 + 1)

        def rows(i):
            return P if i < NT else NS

        def halves(ap):
            return ap.rearrange("p (h r) -> p h r", h=2)

        block = ctx.enter_context(nc.Block())

        @block.sync
        def _(sp):
            def proj_cols(name, lo, hi):
                sp.dma_start(win[:, :, lo:hi], w_in[0, :, lo:hi].rearrange("(k p) n -> p k n", p=P)
                             ).then_inc(ld[name], 16)
            c0 = POOLW + 3 * ATTW
            sp.dma_start(xt[:, 0:4], xT[:, 0:4]).then_inc(ld["xt"], 16)
            proj_cols("gate0", c0 + CONVW, c0 + CONVW + P)
            sp.dma_start(xt[:, 4:8], xT[:, 4:8]).then_inc(ld["xt"], 16)
            proj_cols("a0", c0, c0 + P)
            sp.dma_start(chan[:, :], o["chan"]).then_inc(ld["chan"], 16)
            for i in (1, 2):
                proj_cols(f"gate{i}", c0 + CONVW + i * P, c0 + CONVW + (i + 1) * P)
                proj_cols(f"a{i}", c0 + i * P, c0 + (i + 1) * P)
            proj_cols("k", POOLW + ATTW, POOLW + 2 * ATTW)
            proj_cols("q", POOLW, POOLW + ATTW)
            proj_cols("v", POOLW + 2 * ATTW, POOLW + 3 * ATTW)
            proj_cols("pool", 0, POOLW)
            for lo, hi, t, step in ((0, P, 0, 1), (0, 96, 1, 4), (96, P, 1, 16)):
                first = {1: PAST - P, 4: 512, 16: 0}[step]
                sp.dma_start(kc[lo:hi, :, t, :],
                             cache_k[:, first:first + step * (hi - lo):step, :].rearrange("b p f -> p b f")
                             ).then_inc(ld["kc"], 16)
            for i in range(NT):
                emptied(sp, f"v{i}")
                sp.dma_start(o["p_v"][0, 0, i * P:(i + 1) * P].rearrange("r h d -> r (h d)"), v[:, i]
                             ).then_inc(stored, 16)
            emptied(sp, f"v{NT}")
            sp.dma_start(o["s_v"][0, :, 0].rearrange("b h d -> b (h d)"), v[0:NS, NT]).then_inc(stored, 16)
            stepped(sp, "pool1")
            for lo, hi, t, step in ((0, P, 0, 1), (0, 96, 1, 4), (96, P, 1, 16)):
                first = {1: PAST - P, 4: 512, 16: 0}[step]
                sp.dma_start(vc[lo:hi, :, t, :],
                             cache_v[:, first:first + step * (hi - lo):step, :].rearrange("b p f -> p b f")
                             ).then_inc(ld["vc"], 16)
            sp.dma_start(wo, w_o[0].rearrange("(k p) n -> p k n", p=P)).then_inc(ld["wo"], 16)
            sp.dma_start(l1g, o["ln1_g"].partition_broadcast(P)).then_inc(ld["l1"], 16)
            sp.dma_start(l1b, o["ln1_b"].partition_broadcast(P)).then_inc(ld["l1"], 16)
            for i in range(NT):
                emptied(sp, f"kt{i}")
                sp.dma_start(o["p_k"][0, 0, i * P:(i + 1) * P].rearrange("r h d -> r (h d)"), ktok[:, i % 2]
                             ).then_inc(k_stored[i % 2], 16)
            emptied(sp, "ks")
            sp.dma_start(o["s_k"][0, :, 0].rearrange("b h d -> b (h d)"), ksam).then_inc(k_stored[0], 16)
            emptied(sp, "states")
            keep_p, keep_c = PBUF, CBUF
            sp.dma_start(o["p_pool"][0, 0], st[0:keep_p, 0:POOLW]).then_inc(stored, 16)
            sp.dma_start(o["s_pool"][0, :, keep_p - 1], st[keep_p:keep_p + NS, 0:POOLW]).then_inc(stored, 16)
            sp.dma_start(o["p_conv"][0, 0], st[0:keep_c, POOLW:]).then_inc(stored, 16)
            sp.dma_start(o["s_conv"][0, :, keep_c - 1], st[keep_c:keep_c + NS, POOLW:]).then_inc(stored, 16)
            sp.wait_ge(scored, 1)
            sp.dma_start(pb, o["pbias"]).then_inc(ld["pb"], 16)
            sp.wait_ge(conv_out, 1)
            sp.dma_start(bout, o["e_bout"][0]).then_inc(ld["bout"], 16)
            stepped(sp, "sy")
            stepped(sp, "pv2")
            sp.wait_ge(exp_done, nsteps)
            sp.wait_ge(normed, nsteps)
            for c in (2, 3, 4, 5):
                load_chunk(sp, 0, c)
            stepped(sp, f"wo{NT}")
            for c in (0, 1):
                load_chunk(sp, 0, c)
            sp.wait_ge(stored, 16 * (NT + 1 + 4))
            sp.wait_ge(copied, 32)

        @block.gpsimd
        def _(gp):
            ch = Chain(gp, pool)
            nc.gpsimd.memset(u[:, :, 0:CBUF], 0.0).then_inc(zeroed, 1)
            nc.gpsimd.memset(up[:, :, 0:PBUF], 0.0).then_inc(zeroed, 1)
            nc.gpsimd.memset(memb[:, :, :], 0.0).then_inc(zeroed, 1)
            nc.gpsimd.memset(gates[:, :, :], 0.0).then_inc(zeroed, 1)
            def load_rows(i):
                src = x_prompt[0, i * P:(i + 1) * P] if i < NT else x_sample[:, 0]
                gp.dma_start(xtok[0:rows(i), i % 2], src).then_inc(ld[f"xr{i % 2}"], 16)

            gp.wait_ge(k_stored[0], 48)
            gp.wait_ge(k_stored[1], 32)
            gp.wait_ge(sn_done, 1)
            load_rows(0)
            load_rows(1)
            for n in range(nsteps):
                gp.wait_ge(s_recip, n + 1)
                w = (n % NT + 1) * P
                nc.gpsimd.tensor_scalar(pr[:, n % 2, 0:w], pr[:, n % 2, 0:w], negm[:, 3, n:n + 1], None, ALU.mult
                                        ).then_inc(normed, 1)
            gp.wait_ge(conv_out, 1)
            nc.gpsimd.memset(zero, 0.0).then_inc(zero_made, 1)
            gp.wait_ge(ld["l1"], 32)
            for i in range(NT + 1):
                m = rows(i)
                gp.wait_ge(x_scaled, i + 1)
                if i < NT - 1:
                    load_rows(i + 2)
                nc.gpsimd.tensor_tensor(x1[0:m, i % 2], x1[0:m, i % 2], l1b[0:m], ALU.add).then_inc(x1_ready, 1)

        @block.scalar
        def _(a):
            def small_load(name, dst, src):
                a.dma_start(dst, src).then_inc(ld[name], 16)
            small_load("cst", o["cst"][:, :], o["consts"])
            small_load("ranks", o["slot_rank"][:, :], o["ranks"])
            small_load("ppre", ppre[:, :, :, :], o["pool_prefix"])
            small_load("cpre", cpre[:, :, :, :], o["conv_prefix"])
            small_load("pw", pw[:, :, :], o["pool_w"])
            small_load("rw", rw[:, :, :], o["router_w"])
            small_load("rb", rb[:, :], o["router_b"])
            small_load("bin", binT[:, :, :], o["e_bin"])
            a.dma_start(o["s_pool"][0, :, 0:PBUF - 1], state_pool[0, :, 1:PBUF]).then_inc(copied, 16)
            a.dma_start(o["s_conv"][0, :, 0:CBUF - 1], state_conv[0, :, 1:CBUF]).then_inc(copied, 16)

            def evac(name, dst, src, scale=1.0, func=ACT.Copy):
                stepped(a, name)
                nc.scalar.activation(dst, src, func, scale=scale).then_inc(freed(name), 1)

            for i in range(3):
                evac(f"gate{i}", halves(sig[:, i]), bank(f"gate{i}")[:, :, 0:HALF], func=ACT.Sigmoid)
            for i in range(3):
                evac(f"k{i}", halves(kT[:, i]), bank(f"k{i}")[:, :, 0:HALF])
            for i in range(3):
                evac(f"q{i}", halves(qT[:, i]), bank(f"q{i}")[:, :, 0:HALF], scale=HD ** -0.5)
            for i in range(NT + 1):
                evac(f"v{i}", v[0:rows(i), i], bank(f"v{i}")[0:rows(i), 0, 0:ATTW])
            for i in range(2):
                evac(f"pool{i}", halves(up[:, i, PBUF:]), bank(f"pool{i}")[:, :, 0:HALF])
            for i in range(NT):
                if i >= 2:
                    a.wait_ge(k_stored[i % 2], 16)
                evac(f"kt{i}", ktok[:, i % 2], bank(f"kt{i}")[:, 0, 0:ATTW])
            evac("ks", ksam, bank("ks")[0:NS, 0, 0:ATTW])
            evac("qs", qsam, bank("qs")[0:NS, 0, 0:ATTW])
            stepped(a, "states")
            nc.scalar.activation(st[0:PBUF + NS, 0:POOLW], bank("states")[0:PBUF + NS, 0, 0:POOLW], ACT.Copy
                                 ).then_inc(act, 1)
            evac("states", st[:, POOLW:], bank("states")[0:CBUF + NS, 1, 0:CONVW])
            a.wait_ge(centered, 1)
            nc.scalar.activation(sig[:, :, :], cy[:, :, :], ACT.Square).then_inc(squared, 1)
            emptied(a, "var")
            nc.scalar.activation(rst, rst, ACT.Sqrt).then_inc(rst_done, 1)
            for i in range(3):
                a.wait_ge(z_done, i + 1)
                nc.scalar.activation(sig[:, i], cy[:, i], ACT.Sigmoid, scale=chn("cg")[:, i:i + 1],
                                     bias=chn("cbeta")[:, i:i + 1]).then_inc(swish, 1)
            for i in range(2):
                evac(f"pw{i}", halves(mix[:, i]), bank(f"pw{i}")[:, :, 0:HALF], scale=chn("ps")[:, i:i + 1])
            a.wait_ge(s_neg, 1)
            nc.scalar.activation(s48[:, :], s48[:, :], ACT.Exp, bias=col48[:, 3:4], accum_out=col48[:, 4:5]
                                 ).then_inc(s_exp, 1)
            evac("pst", ps48[:, :, :], bank("pst")[:, 0, 0:2 * NH * NS].rearrange("p (t c) -> p t c", t=2))
            evac("snew2", dnew[:, :, :], bank("snew2")[0:NS, 0, 0:NH * NS].rearrange("p (h b) -> p h b", h=NH))
            stepped(a, "sy")
            sy = bank("sy")[:, 0, 0:3 * 2 * NS].rearrange("p (g b j) -> p g b j", g=3, j=2)
            nc.scalar.activation(mix[0:HD, 2:5, SEQ:R], sy[0:HD, :, :, 0], ACT.Copy).then_inc(act, 1)
            nc.scalar.activation(mix[HD:P, 2:5, SEQ:R], sy[HD:P, :, :, 1], ACT.Copy).then_inc(freed("sy"), 1)
            for n in range(nsteps + 3):
                if n < nsteps:
                    w = (n % NT + 1) * P
                    a.wait_ge(s_max, n + 1)
                    if n >= 2:
                        a.wait_ge(tr_done, n - 1)
                    nc.scalar.activation(pr[:, n % 2, 0:w], sc[:, n % 2, 0:w], ACT.Exp,
                                         bias=negm[:, 1, n:n + 1], accum_out=negm[:, 2, n:n + 1]
                                         ).then_inc(exp_done, 1)
                if n >= 3:
                    m = n - 3
                    h, i = divmod(m, NT)
                    a.wait_ge(tr_done, m + 1)
                    if h >= 2 and i == 0:
                        if h % 2 == 0:
                            a.wait_ge(pv_even, h // 2)
                        else:
                            stepped(a, f"pv{(h - 2) // 2}")
                    nc.scalar.activation(pt[:, h % 2, 0:i + 1, i * P:(i + 1) * P],
                                         bT[m % 2][:, 0:(i + 1) * P].rearrange("p (j q) -> p j q", q=P),
                                         ACT.Copy).then_inc(pt_done, 1)
                    if i == NT - 1 and h % 2 == 1 and h >= 3:
                        hp = h // 2 - 1
                        evac(f"pv{hp}", mix[:, 2 + hp, 0:SEQ], bank(f"pv{hp}")[:, 0])
            evac("pv2", mix[:, 4, 0:SEQ], bank("pv2")[:, 0])
            def ln1_root(i):
                a.wait_ge(var_ready, i + 1)
                nc.scalar.activation(mv[0:rows(i), 3:4], mv[0:rows(i), 1:2], ACT.Sqrt).then_inc(rstd_ready, 1)
            ln1_root(0)
            ln1_root(1)
            for i in range(NT + 1):
                m = rows(i)
                a.wait_ge(x1_ready, i + 1)
                a.dma_start(x1_dram[i * P:i * P + m], x1[0:m, i % 2]).then_inc(x1_sent[i % 2], 16)
                for q in range(2):
                    a.wait_ge(x1T_done, 2 * i + q + 1)
                    nc.scalar.activation(x1t[:, i % 2, 4 * q:4 * q + 4, 0:m],
                                         bT[q][:, 0:4 * m].rearrange("p (k r) -> p k r", k=4), ACT.Copy
                                         ).then_inc(x1T_ready, 1)
                a.wait_ge(top_neg, i + 1)
                nc.scalar.activation(tf[0:m, 4:8], top[0:m, 0:4], ACT.Exp, bias=tf[0:m, 8:9],
                                     accum_out=tf[0:m, 9:10]).then_inc(top_exp, 1)
                a.wait_ge(gT_done, i + 1)
                nc.scalar.activation(gT[:, 0:m], bS[1][0:NE, 0:m], ACT.Copy).then_inc(gT_ready, 1)
                if i < 3:
                    ln1_root(i + 2)
                a.wait_ge(acc_ready, i + 1)
                a.dma_start(acc_dram[i * P:i * P + m], accs[0:m]).then_inc(acc_sent, 16)
            a.wait_ge(zero_made, 1)
            for q in range(CAP // P):
                for c in range(4):
                    a.dma_start(acc_dram[PAD0 + q * P:PAD0 + (q + 1) * P, c * (D // 4):(c + 1) * (D // 4)], zero
                                ).then_inc(acc_sent, 16)
            a.wait_ge(acc_sent, 16 * (NT + 1 + 4 * (CAP // P)))
            a.wait_ge(x1_sent[0], 48)
            a.wait_ge(x1_sent[1], 32)

        @block.tensor
        def _(pe):
            def begin(name):
                if STEP[name] >= 2:
                    pe.wait_ge(freed(name), STEP[name] // 2)
                return bank(name)

            def project(name, lo, waits):
                b = begin(name)
                for s in waits:
                    pe.wait_ge(*s)
                for h in range(2):
                    for k in range(KT):
                        mm = nc.tensor.matmul(b[:, h, 0:HALF], win[:, k, lo:lo + P],
                                              xt[:, k, h * HALF:(h + 1) * HALF], start=k == 0, stop=k == KT - 1)
                mm.then_inc(pe_step, 1)

            c0 = POOLW + 3 * ATTW
            pe.wait_ge(ld["xt"], 32)
            for i in range(3):
                project(f"gate{i}", c0 + CONVW + i * P, [(ld[f"gate{i}"], 16)])
                project(f"a{i}", c0 + i * P, [(ld[f"a{i}"], 16)])
            for i in range(3):
                project(f"k{i}", POOLW + ATTW + i * P, [(ld["k"], 16)])
            for i in range(3):
                project(f"q{i}", POOLW + i * P, [(ld["q"], 16)])
            pe.wait_ge(ld["v"], 16)
            for i in range(NT + 1):
                b = begin(f"v{i}")
                for k in range(KT):
                    mm = nc.tensor.matmul(b[0:rows(i), 0, 0:ATTW], xt[:, k, i * P:i * P + rows(i)],
                                          win[:, k, POOLW + 2 * ATTW:POOLW + 3 * ATTW],
                                          start=k == 0, stop=k == KT - 1)
                mm.then_inc(pe_step, 1)
            for i in range(2):
                project(f"pool{i}", i * P, [(ld["pool"], 16)])
            pe.wait_ge(ld["cst"], 16)
            emptied(pe, "k2")
            emptied(pe, "q2")
            for i in range(NT):
                b = begin(f"kt{i}")
                for f in range(3):
                    mm = nc.tensor.transpose(b[:, 0, f * P:(f + 1) * P], kT[:, f, i * P:(i + 1) * P], C("ident"))
                mm.then_inc(pe_step, 1)
            for name, src in (("ks", kT), ("qs", qT)):
                b = begin(name)
                for f in range(3):
                    mm = nc.tensor.transpose(b[0:NS, 0, f * P:(f + 1) * P], src[:, f, SEQ:R], C("ident"))
                mm.then_inc(pe_step, 1)
            b = begin("states")
            emptied(pe, "pool1")
            emptied(pe, "a2")
            for f in range(2):
                nc.tensor.transpose(b[0:PBUF + NS, 0, f * P:(f + 1) * P], up[:, f, SEQ:PBUF + R], C("ident"))
            for f in range(3):
                mm = nc.tensor.transpose(b[0:CBUF + NS, 1, f * P:(f + 1) * P], u[:, f, SEQ:CBUF + R], C("ident"))
            mm.then_inc(pe_step, 1)
            for name, src, s in (("mean", cy, conv_done), ("var", sig, squared)):
                b = begin(name)
                pe.wait_ge(s, 1)
                for h in range(2):
                    for i in range(3):
                        mm = nc.tensor.matmul(b[:, h, 0:HALF], C("mean"), src[:, i, h * HALF:(h + 1) * HALF],
                                              start=i == 0, stop=i == 2)
                mm.then_inc(pe_step, 1)
            pe.wait_ge(pool_d, 1)
            pe.wait_ge(ld["pw"], 16)
            for i in range(2):
                b = begin(f"pw{i}")
                for h in range(2):
                    mm = nc.tensor.matmul(b[:, h, 0:HALF], pw[:, i], scr2[:, i, h * HALF:(h + 1) * HALF],
                                          start=True, stop=True)
                mm.then_inc(pe_step, 1)
            emptied(pe, "qs")
            for s in range(NS):
                b = begin(f"qb{s}")
                nc.tensor.matmul(b[:, 0, 0:ATTW], C("sel", NS)[:, s * P:(s + 1) * P], qsam, start=True, stop=True
                                 ).then_inc(pe_step, 1)
            b = begin("snew")
            pe.wait_ge(sn_done, 1)
            nc.tensor.matmul(b[0:NH * NS, 0, 0:NH], C("spread", NS), sn[:, :], start=True, stop=True
                             ).then_inc(pe_step, 1)
            b = begin("st")
            pe.wait_ge(scored, 1)
            for t in range(2):
                mm = nc.tensor.transpose(b[0:NH * NS, 0, t * P:(t + 1) * P], ssc[:, t], C("ident"))
            mm.then_inc(pe_step, 1)

            def sample_probs():
                b = begin("pst")
                pe.wait_ge(s_prob, 2)
                for t in range(2):
                    mm = nc.tensor.transpose(b[:, 0, t * NH * NS:(t + 1) * NH * NS], s48[:, t * P:(t + 1) * P],
                                             C("ident", NH * NS)[:, 0:NH * NS])
                mm.then_inc(pe_step, 1)
                b = begin("snew2")
                nc.tensor.matmul(b[0:NS, 0, 0:NH * NS], C("gather", NH * NS), dg48[:, :], start=True, stop=True
                                 ).then_inc(pe_step, 1)

            def sample_values():
                b = begin("sy")
                emptied(pe, "snew2")
                emptied(pe, "pst")
                pe.wait_ge(ld["vc"], 48)
                sy = b[:, 0, 0:3 * 2 * NS].rearrange("p (g b j) -> p g b j", g=3, j=2)
                for g in range(3):
                    nc.tensor.matmul(sy[:, g], v[0:NS, NT, g * P:(g + 1) * P],
                                     dnew[:, 2 * g:2 * g + 2, :].rearrange("p j b -> p b j"), start=True, stop=False,
                                     skip_group_check=True)
                    for s in range(NS):
                        for t in range(2):
                            mm = nc.tensor.matmul(sy[:, g, s], vc[:, s, t, g * P:(g + 1) * P],
                                                  ps48[:, t, s * NH + 2 * g:s * NH + 2 * g + 2],
                                                  start=False, stop=(s == NS - 1 and t == 1),
                                                  skip_group_check=True)
                mm.then_inc(pe_step, 1)

            def scores(n):
                h, i = divmod(n, NT)
                lo = HD * (h % 2)
                if n >= 2:
                    pe.wait_ge(s_max, n - 1)
                nc.tensor.matmul(bS[n % 2][:, 0:(i + 1) * P], qT[lo:lo + HD, h // 2, i * P:(i + 1) * P],
                                 kT[lo:lo + HD, h // 2, 0:(i + 1) * P], start=True, stop=True
                                 ).then_inc(qk_done, 1)

            def turn(n):
                i = n % NT
                pe.wait_ge(normed, n + 1)
                if n >= 2:
                    pe.wait_ge(pt_done, n - 1)
                for j in range(i + 1):
                    mm = nc.tensor.transpose(bT[n % 2][:, j * P:(j + 1) * P], pr[:, n % 2, j * P:(j + 1) * P],
                                             C("ident"))
                mm.then_inc(tr_done, 1)

            def values(h):
                b = begin(f"pv{h // 2}") if h % 2 == 0 else bank(f"pv{h // 2}")
                lo = HD * (h % 2)
                pe.wait_ge(pt_done, NT * (h + 1))
                for j in range(NT):
                    mm = nc.tensor.matmul(b[lo:lo + HD, 0, j * P:SEQ], v[:, j, h * HD:(h + 1) * HD],
                                          pt[:, h % 2, j, j * P:SEQ], start=j == 0, stop=j == NT - 1)
                mm.then_inc(pe_step if h % 2 else pv_even, 1)

            sample_probs()
            sample_values()
            for n in range(nsteps + 4):
                if n < nsteps:
                    scores(n)
                if 2 <= n < nsteps + 2:
                    turn(n - 2)
                if n >= 4 and (n - 4) % NT == NT - 1:
                    values((n - 4) // NT)

            def out_proj(i):
                b = begin(f"wo{i}")
                for h in range(2):
                    for k in range(KT):
                        mm = nc.tensor.matmul(b[0:rows(i), h], mix[:, k, i * P:i * P + rows(i)],
                                              wo[:, k, h * 512:(h + 1) * 512], start=k == 0, stop=k == KT - 1)
                mm.then_inc(pe_step, 1)

            def router(i):
                m = rows(i)
                pe.wait_ge(x1_ready, i + 1)
                for q in range(2):
                    if i >= 1:
                        pe.wait_ge(x1T_ready, 2 * i - 1 + q)
                    for k in range(4):
                        mm = nc.tensor.transpose(bT[q][:, k * m:(k + 1) * m], x1[0:m, i % 2, (4 * q + k) * P:(4 * q + k + 1) * P],
                                                 C("ident", m)[:, 0:m])
                    mm.then_inc(x1T_done, 1)
                if i >= 1:
                    pe.wait_ge(top_neg, i)
                nc.tensor.matmul(bS[0][0:m, 0:NE], C("ones", 1)[:, 0:m], rb[:, :], start=True, stop=False)
                for k in range(KT):
                    if k % 4 == 0:
                        pe.wait_ge(x1T_ready, 2 * i + k // 4 + 1)
                    mm = nc.tensor.matmul(bS[0][0:m, 0:NE], x1t[:, i % 2, k, 0:m], rw[:, k], start=False,
                                          stop=k == KT - 1)
                mm.then_inc(lg_done, 1)

            def expert_bias(i):
                m = rows(i)
                pe.wait_ge(g_ready, i + 1)
                if i >= 1:
                    pe.wait_ge(gT_ready, i)
                nc.tensor.transpose(bS[1][0:NE, 0:m], gates[0:m, i], C("ident", m)[:, 0:m]).then_inc(gT_done, 1)
                b = begin(f"bo{i}")
                pe.wait_ge(gT_ready, i + 1)
                for h in range(2):
                    mm = nc.tensor.matmul(b[0:m, h], gT[:, 0:m], bout[:, h * 512:(h + 1) * 512], start=True, stop=True)
                mm.then_inc(pe_step, 1)

            emptied(pe, "pw1")
            emptied(pe, "sy")
            emptied(pe, "pv2")
            pe.wait_ge(conv_out, 1)
            pe.wait_ge(ld["wo"], 16)
            out_proj(0)
            out_proj(1)
            pe.wait_ge(ld["rw"], 16)
            pe.wait_ge(ld["rb"], 16)
            pe.wait_ge(ld["bout"], 16)
            for i in range(NT + 1):
                router(i)
                expert_bias(i) if i < NT - 1 + 1 and i < 3 else None
                if i < 3:
                    out_proj(i + 2)
                else:
                    expert_bias(i)
            pe.wait_ge(m_ready, NT + 1)
            for i in range(NT + 1):
                for j in range(i + 1):
                    nc.tensor.matmul(bS[0][:, i * NE:(i + 1) * NE], C("tri" if j == i else "ones", rows(j)),
                                     memb[0:rows(j), j], start=j == 0, stop=j == i)
            for j in range(NT + 1):
                mm = nc.tensor.matmul(bS[0][:, (NT + 1) * NE:(NT + 2) * NE], C("ones", rows(j)), memb[0:rows(j), j],
                                      start=j == 0, stop=j == NT)
            mm.then_inc(rank_done, 1)

        @block.vector
        def _(d):
            V = nc.vector
            ch = Chain(d, dve)
            d.wait_ge(zeroed, 4)
            for i in range(3):
                stepped(d, f"a{i}")
                emptied(d, f"gate{i}")
                V.tensor_tensor(halves(u[:, i, CBUF:]), bank(f"a{i}")[:, :, 0:HALF], halves(sig[:, i]), ALU.mult
                                ).then_inc(freed(f"a{i}"), 1)
            emptied(d, "a2")
            d.wait_ge(ld["chan"], 16)
            d.wait_ge(ld["cpre"], 16)
            d.wait_ge(ld["ppre"], 16)
            d.wait_ge(ld["cst"], 16)
            d.wait_ge(ld["ranks"], 16)
            for i in range(3):
                ch.mark(V.tensor_scalar(cy[:, i, 0:SEQ], u[:, i, 0:SEQ], taps[:, i, 0:1], chn("cb")[:, i:i + 1],
                                        ALU.mult, ALU.add))
            for t in range(1, TAPS):
                for i in range(3):
                    ch.wait(ch.n - 2)
                    ch.mark(V.scalar_tensor_tensor(cy[:, i, 0:SEQ], u[:, i, t:t + SEQ], taps[:, i, t:t + 1],
                                                   cy[:, i, 0:SEQ], ALU.mult, ALU.add))
            pre = sig[:, :, 0:NS * CBUF].rearrange("p i (b t) -> p i b t", b=NS)
            for i in range(3):
                ch.mark(V.tensor_tensor(pre[:, i], cpre[:, i], taps[:, i, 0:CBUF].unsqueeze(1).broadcast_to([P, NS, CBUF]),
                                        ALU.mult))
            ch.wait()
            ch.do(V.tensor_reduce(conv8[:, :, :], pre, AX.X, ALU.add))
            for i in range(3):
                ch.mark(V.scalar_tensor_tensor(conv8[:, i], u[:, i, CBUF + SEQ:], taps[:, i, CBUF:TAPS], conv8[:, i],
                                               ALU.mult, ALU.add))
            ch.wait()
            for i in range(3):
                ins = V.tensor_scalar(cy[:, i, SEQ:R], conv8[:, i], chn("cb")[:, i:i + 1], None, ALU.add)
                (ch.mark(ins) if i < 2 else ins.then_inc(conv_done, 1))
            emptied(d, "pool1")
            ch.do(V.tensor_tensor(scr[:, :, 0:SEQ], up[:, :, PBUF:PBUF + SEQ], up[:, :, PBUF - 1:PBUF - 1 + SEQ], ALU.add))
            def double(lo, i, src, dst, w):
                p = slice(lo, P)
                ch.mark(V.tensor_tensor(dst[p, i, w:SEQ], src[p, i, w:SEQ], src[p, i, 0:SEQ - w], ALU.add))
                ch.do(V.tensor_copy(dst[p, i, 0:w], src[p, i, 0:w]))
            double(HD, 0, scr, scr2, 2)
            ch.do(V.tensor_copy(scr2[0:HD, 0, 0:SEQ], scr[0:HD, 0, 0:SEQ]))
            double(0, 1, scr, scr2, 2)
            double(0, 1, scr2, scr, 4)
            ch.do(V.tensor_copy(scr2[0:HD, 1, 0:SEQ], scr[0:HD, 1, 0:SEQ]))
            double(HD, 1, scr, scr2, 8)
            cnt = C("cnt").rearrange("p (i t) -> p i t", i=2)
            ch.do(V.tensor_tensor(scr[:, :, 0:PBUF], scr2[:, :, 0:PBUF], cnt, ALU.mult))
            for i in range(2):
                ch.mark(V.scalar_tensor_tensor(scr2[:, i, PBUF:SEQ], scr2[:, i, PBUF:SEQ], C("invw")[:, i:i + 1],
                                               up[:, i, 2 * PBUF:PBUF + SEQ], ALU.mult, ALU.subtract))
            ch.mark(V.tensor_tensor(scr2[:, :, 0:PBUF], scr[:, :, 0:PBUF], up[:, :, PBUF:2 * PBUF], ALU.subtract))
            wm = C("wmask").rearrange("p (i t) -> p i t", i=2)
            pre = scr[:, :, 0:NS * PBUF].rearrange("p i (b t) -> p i b t", b=NS)
            ch.wait()
            for i in range(2):
                ch.mark(V.tensor_tensor(pre[:, i], ppre[:, i], wm[:, i].unsqueeze(1).broadcast_to([P, NS, PBUF]), ALU.mult))
            ch.wait()
            ch.do(V.tensor_reduce(pool8[:, :, :], pre, AX.X, ALU.add))
            ch.do(V.tensor_tensor(pool8[:, :, :], pool8[:, :, :], up[:, :, PBUF + SEQ:], ALU.add))
            for i in range(2):
                ins = V.scalar_tensor_tensor(scr2[:, i, SEQ:R], pool8[:, i], C("invw")[:, i:i + 1],
                                             up[:, i, PBUF + SEQ:], ALU.mult, ALU.subtract)
                (ch.mark(ins) if i == 0 else ins.then_inc(pool_d, 1))
            stepped(d, "mean")
            d.wait_ge(conv_done, 1)
            for i in range(3):
                ins = V.tensor_tensor(halves(cy[:, i]), halves(cy[:, i]), bank("mean")[:, :, 0:HALF], ALU.subtract)
                (ch.mark(ins) if i < 2 else ins.then_inc(freed("mean"), 1))
            emptied(d, "mean")
            ch.wait()
            d.engine_nop().then_inc(centered, 1)
            def sample_scores(s):
                stepped(d, f"qb{s}")
                if s == 0:
                    d.wait_ge(ld["kc"], 48)
                ins = V.tensor_tensor(prod, kc[:, s], bank(f"qb{s}")[:, 0, 0:ATTW].unsqueeze(1).broadcast_to([P, 2, ATTW]),
                                      ALU.mult)
                ins.then_inc(freed(f"qb{s}"), 1)
                emptied(d, f"qb{s}")
                return V.tensor_reduce(ssc[:, :, s * NH:(s + 1) * NH], prod.rearrange("p t (h e) -> p t h e", e=HD),
                                       AX.X, ALU.add)
            stepped(d, "var")
            V.tensor_scalar(halves(rst), bank("var")[:, :, 0:HALF], EPS, None, ALU.add).then_inc(freed("var"), 1)
            d.wait_ge(rst_done, 1)
            ch.do(V.reciprocal(rst, rst))
            for i in range(3):
                V.tensor_tensor(cy[:, i], cy[:, i], rst, ALU.mult).then_inc(z_done, 1)
            stepped(d, "pw1")
            for i in range(3):
                d.wait_ge(swish, i + 1)
                ch.mark(V.tensor_scalar(cy[:, i], cy[:, i], chn("cg")[:, i:i + 1], chn("cbeta")[:, i:i + 1],
                                        ALU.mult, ALU.add))
            ch.wait()
            for i in range(3):
                ins = V.tensor_tensor(mix[:, 5 + i], cy[:, i], sig[:, i], ALU.mult)
                (ch.mark(ins) if i < 2 else ins.then_inc(conv_out, 1))
            d.wait_ge(conv_out, 1)
            for s in range(NS):
                ins = sample_scores(s)
                (ch.do(ins) if s < NS - 1 else ins.then_inc(scored, 1))
            d.wait_ge(scored, 1)
            emptied(d, "ks")
            emptied(d, "qs")
            p8 = prod[0:NS, 0]
            ch.do(V.tensor_tensor(p8, qsam, ksam, ALU.mult))
            V.tensor_reduce(sn[:, :], p8.rearrange("p (h e) -> p h e", e=HD), AX.X, ALU.add).then_inc(sn_done, 1)
            stepped(d, "snew")
            V.tensor_tensor_reduce(dg48[:, 0:NH], bank("snew")[0:NH * NS, 0, 0:NH], C("headof", NH * NS), 1.0, 0.0,
                                   ALU.mult, ALU.add, col48[:, 0:1]).then_inc(freed("snew"), 1)
            stepped(d, "st")
            V.tensor_tensor_reduce(s48[:, 0:2 * P], bank("st")[0:NH * NS, 0, 0:2 * P], C("sbias", NH * NS)[:, 0:2 * P],
                                   1.0, MASKED * 4, ALU.add, ALU.max, col48[:, 1:2]).then_inc(freed("st"), 1)
            emptied(d, "snew")
            ch.do(V.tensor_tensor(s48[:, 2 * P:], col48[:, 0:1], C("sbias", NH * NS)[:, 2 * P:], ALU.add))
            emptied(d, "st")
            ch.do(V.tensor_tensor(col48[:, 2:3], col48[:, 1:2], s48[:, 2 * P:], ALU.max))
            V.tensor_scalar(col48[:, 3:4], col48[:, 2:3], -1.0, None, ALU.mult).then_inc(s_neg, 1)
            d.wait_ge(s_exp, 1)
            ch.do(V.reciprocal(col48[:, 5:6], col48[:, 4:5]))
            V.tensor_scalar(s48[:, :], s48[:, :], col48[:, 5:6], None, ALU.mult).then_inc(s_prob, 1)
            d.wait_ge(s_prob, 1)
            V.tensor_scalar(dg48[:, :], C("diag", NH * NS), s48[:, 2 * P:], None, ALU.mult).then_inc(s_prob, 1)
            d.wait_ge(ld["pb"], 16)
            for n in range(nsteps + 1):
                if n < nsteps:
                    h, i = divmod(n, NT)
                    w = (i + 1) * P
                    d.wait_ge(qk_done, n + 1)
                    if n >= 2:
                        d.wait_ge(exp_done, n - 1)
                    ch.do(V.tensor_tensor_reduce(sc[:, n % 2, 0:w], bS[n % 2][:, 0:w], pb[:, h, SEQ - w:SEQ], 1.0,
                                                 MASKED * 4, ALU.add, ALU.max, negm[:, 0, n:n + 1]))
                    V.tensor_scalar(negm[:, 1, n:n + 1], negm[:, 0, n:n + 1], -1.0, None, ALU.mult).then_inc(s_max, 1)
                if n >= 1:
                    d.wait_ge(exp_done, n)
                    V.reciprocal(negm[:, 3, n - 1:n], negm[:, 2, n - 1:n]).then_inc(s_recip, 1)
            def ln1(i):
                m = rows(i)
                stepped(d, f"wo{i}")
                d.wait_ge(ld[f"xr{i % 2}"], 16 * (i // 2 + 1))
                if i >= 2:
                    d.wait_ge(x1_sent[i % 2], 16 * (i // 2))
                    stepped(d, f"bo{i - 2}")
                xr = x1[0:m, i % 2]
                V.scalar_tensor_tensor(xr, xtok[0:m, i % 2], ALPHA_N,
                                       bank(f"wo{i}")[0:m].rearrange("p h n -> p (h n)"), ALU.mult, ALU.add
                                       ).then_inc(freed(f"wo{i}"), 1)
                emptied(d, f"wo{i}")
                for h in range(2):
                    ch.mark(V.bn_stats(bn[0:m, h], xr[:, h * 512:(h + 1) * 512]))
                ch.wait()
                ch.do(V.bn_aggr(mv[0:m, 0:2], bn[0:m].rearrange("p h s -> p (h s)")))
                V.tensor_scalar(mv[0:m, 1:2], mv[0:m, 1:2], EPS, None, ALU.add).then_inc(var_ready, 1)
                d.wait_ge(rstd_ready, i + 1)
                ch.do(V.reciprocal(mv[0:m, 2:3], mv[0:m, 3:4]))
                ch.do(V.tensor_scalar(xr, xr, mv[0:m, 0:1], mv[0:m, 2:3], ALU.subtract, ALU.mult))
                if i == 0:
                    d.wait_ge(ld["l1"], 32)
                V.tensor_tensor(xr, xr, l1g[0:m], ALU.mult).then_inc(x_scaled, 1)

            def route(i):
                m = rows(i)
                d.wait_ge(lg_done, i + 1)
                ch.do(V.tensor_copy(lg[0:m], bS[0][0:m, 0:NE]))
                ch.do(V.max(top[0:m], lg[0:m]))
                V.tensor_scalar(tf[0:m, 8:9], top[0:m, 0:1], -1.0, None, ALU.mult).then_inc(top_neg, 1)
                ch.do(V.max_index(topi[0:m], top[0:m], lg[0:m]))
                ch.do(V.tensor_copy(tf[0:m, 0:4], topi[0:m, 0:4]))
                ch.do(V.tensor_tensor(oh4[0:m], C("exp", m).unsqueeze(1).broadcast_to([m, TOPK, NE]),
                                      tf[0:m, 0:4].unsqueeze(2).broadcast_to([m, TOPK, NE]), ALU.is_equal))
                V.tensor_reduce(memb[0:m, i], oh4[0:m].rearrange("p k e -> p e k"), AX.X, ALU.add
                                ).then_inc(m_ready, 1)
                d.wait_ge(top_exp, i + 1)
                ch.do(V.reciprocal(tf[0:m, 10:11], tf[0:m, 9:10]))
                ch.do(V.tensor_scalar(tf[0:m, 12:16], tf[0:m, 4:8], tf[0:m, 10:11], None, ALU.mult))
                ch.do(V.tensor_tensor(og4[0:m], oh4[0:m], tf[0:m, 12:16].unsqueeze(2).broadcast_to([m, TOPK, NE]),
                                      ALU.mult))
                V.tensor_reduce(gates[0:m, i], og4[0:m].rearrange("p k e -> p e k"), AX.X, ALU.add
                                ).then_inc(g_ready, 1)

            def acc_start(i):
                m = rows(i)
                stepped(d, f"bo{i}")
                if i >= 1:
                    d.wait_ge(acc_sent, 16 * i)
                d.wait_ge(x1_ready, i + 1)
                V.scalar_tensor_tensor(accs[0:m], x1[0:m, i % 2], ALPHA_N,
                                       bank(f"bo{i}")[0:m].rearrange("p h n -> p (h n)"), ALU.mult, ALU.add
                                       ).then_inc(freed(f"bo{i}"), 1)
                emptied(d, f"bo{i}")
                d.engine_nop().then_inc(acc_ready, 1)

            ln1(0)
            ln1(1)
            for i in range(NT + 1):
                route(i)
                if i < 3:
                    acc_start(i)
                    ln1(i + 2)
                elif i == 3:
                    acc_start(i)
            d.wait_ge(rank_done, 1)
            ch.do(V.tensor_scalar(rankm[:, :, :], memb[:, :, :], -1.0, 1e6, ALU.add, ALU.mult))
            ch.mark(V.tensor_tensor(rankm[:, :, :], rankm[:, :, :],
                                    bS[0][:, 0:(NT + 1) * NE].rearrange("p (i e) -> p i e", e=NE), ALU.add))
            ch.do(V.memset(jf, 0.0))
            row = lambda k: jr[:, k, :]
            CNT, OV, BASE, TMP, TMP2 = range(5)
            ch.do(V.tensor_copy(row(CNT), bS[0][0:1, (NT + 1) * NE:(NT + 2) * NE]))
            ch.mark(V.tensor_scalar(row(OV), row(CNT), float(CAP), None, ALU.is_gt))
            ch.do(V.tensor_scalar(row(TMP), row(CNT), float(2 * CAP), None, ALU.is_gt))
            ch.do(V.tensor_tensor(row(OV), row(OV), row(TMP), ALU.add))
            ch.do(V.tensor_copy(row(TMP), row(OV)))
            a, b, w = TMP, TMP2, 1
            while w < NE:
                ch.mark(V.tensor_copy(jr[:, b, 0:w], jr[:, a, 0:w]))
                ch.do(V.tensor_tensor(jr[:, b, w:], jr[:, a, w:], jr[:, a, 0:NE - w], ALU.add))
                a, b, w = b, a, 2 * w
            ch.mark(V.tensor_scalar(jf[:, 0, NJ:NJ + 1], jr[:, a, NE - 1:], float(NE), None, ALU.add))
            ch.do(V.tensor_tensor(row(BASE), row(a), row(OV), ALU.subtract))
            ch.mark(V.tensor_copy(njobs[:, :], jf[:, 0, NJ:NJ + 1]))
            ch.mark(V.tensor_copy(jf[:, 0, 0:NE], C("exp", 1)))
            ch.mark(V.tensor_scalar(jf[:, 2, 0:NE], row(CNT), float(CAP), None, ALU.min))
            over = lambda k: jv[:, k]
            both = lambda ap: ap.unsqueeze(1).broadcast_to([1, NOVER, NE])
            ch.do(V.tensor_tensor(over(0), C("jobno", 1).unsqueeze(2).broadcast_to([1, NOVER, NE]), both(row(BASE)),
                                  ALU.subtract))
            ch.do(V.tensor_tensor(over(1), over(0), both(row(OV)), ALU.is_lt))
            ch.do(V.tensor_scalar(over(2), over(0), 0.0, None, ALU.is_ge))
            ch.do(V.tensor_tensor(over(1), over(1), over(2), ALU.mult))
            ch.do(V.tensor_tensor(over(2), over(1), both(C("exp", 1)), ALU.mult))
            ch.do(V.tensor_reduce(jf[:, 0, NE:NJ], over(2), AX.X, ALU.add))
            ch.do(V.tensor_scalar(over(0), over(0), 1.0, float(CAP), ALU.add, ALU.mult))
            ch.do(V.tensor_tensor(over(0), over(0), over(1), ALU.mult))
            ch.do(V.tensor_reduce(jf[:, 1, NE:NJ], over(0), AX.X, ALU.add))
            ch.do(V.tensor_tensor(over(2), over(1), both(row(CNT)), ALU.mult))
            ch.do(V.tensor_reduce(jf[:, 2, NE:NJ], over(2), AX.X, ALU.add))
            ch.do(V.tensor_tensor(jf[:, 2, NE:NJ], jf[:, 2, NE:NJ], jf[:, 1, NE:NJ], ALU.subtract))
            ch.do(V.tensor_scalar(jf[:, 2, NE:NJ], jf[:, 2, NE:NJ], float(CAP), None, ALU.min))
            ch.mark(V.tensor_scalar(jf[:, 1, 0:NE], row(CNT), float(FEW), float(TWICE), ALU.is_le, ALU.mult))
            ch.do(V.tensor_scalar(jf[:, 2, NE:NJ], jf[:, 2, NE:NJ], FEW + 1.0, None, ALU.max))
            ch.do(V.memset(jf[:, 0, NJ:], 0.0))
            ch.mark(V.tensor_copy(jobs[:, :, :], jf))
            acc_start(NT)
            ch.wait()


def moe_block(nc, o):
    ring, slot_rank, rankm, gates, jobs, njobs, binT, C, sem, load_chunk, chunk_in = (
        o[k] for k in "ring slot_rank rankm gates jobs njobs binT C sem load_chunk chunk_in".split())
    x1_dram, acc_dram = o["x1_dram"], o["acc_dram"]

    with ExitStack() as ctx:
        def sb(name, shape, dt=F32):
            return ctx.enter_context(nc.sbuf_tensor(name, shape, dt))

        def bsem(name):
            return ctx.enter_context(nc.semaphore(name))

        xg = sb("xg", [P, 2, D])
        xgT = sb("xgT", [P, KT, CAP])
        hid = sb("hid", [P, FT, CAP])
        y = sb("y", [P, 2, D])
        gg = sb("gg", [P, 2, CAP])
        uu = sb("uu", [P, 2, CAP])
        ss = sb("ss", [P, 2, CAP])
        onehot = sb("onehot", [P, NT + 1, CAP], BF16)
        pay = sb("pay", [P, NT + 1, 6], BF16)
        gparts = sb("gparts", [P, NT + 1, NE, 3], BF16)
        grest = sb("grest", [P, NT + 1, NE])
        pads = sb("pads", [P, 2])
        numbers = sb("numbers", [P, 2])
        idx_next = sb("idx_next", [P, 2], I32)
        gate_next = sb("gate_next", [P, 2])
        idx_held = sb("idx_held", [P, 2], I32)
        gate_held = sb("gate_held", [P, 2])
        idx_cur = sb("idx_cur", [P, 2], I32)
        gate_cur = sb("gate_cur", [P, 2])
        jbias = sb("jbias", [P, 2 * FT])
        l2g = sb("l2g", [P, D])
        l2b = sb("l2b", [P, D])
        fin = sb("fin", [P, NT + 1, D])
        bn2 = sb("bn2", [P, 2, 6])
        mv2 = sb("mv2", [P, NT + 1, 4])

        pu = [ctx.enter_context(nc.psum_tensor(f"pu{i}", [P, 2, CAP], F32)) for i in range(2)]
        px = [ctx.enter_context(nc.psum_tensor(f"px{i}", [P, 512], F32)) for i in range(2)]
        py = [[ctx.enter_context(nc.psum_tensor(f"py{h}{c}", [P, 512], F32)) for c in range(2)] for h in range(2)]

        up_done = bsem("up_done")
        pu_free = bsem("pu_free")
        g_ready = bsem("gate_in_sbuf")
        sig_done = bsem("sigmoid_done")
        hid_done = bsem("hid_done")
        onehot_ready = bsem("onehot_ready")
        slots_done = bsem("slots_done")
        slots_ready = bsem("slots_ready")
        cur_ready = bsem("cur_ready")
        gathered = [bsem(f"gathered{h}") for h in range(2)]
        turned = bsem("turned")
        xgT_ready = bsem("xgT_ready")
        down_done = bsem("down_done")
        y_read = [bsem(f"y_read{c}") for c in range(2)]
        scattered = [bsem(f"scattered{h}") for h in range(2)]
        gathers = bsem("gathers")
        y_free = bsem("y_free")
        ready = bsem("constants_ready")
        xg_zero = bsem("xg_zero")
        ln2_in = bsem("ln2_in")
        acc_in = [bsem(f"acc_in{i}") for i in range(NT + 1)]
        scaled2 = bsem("scaled2")
        var2 = bsem("ln2_var_ready")
        rstd2 = bsem("ln2_rstd_ready")
        y_ready = bsem("y_ready")
        y_out = bsem("y_out")
        dve = bsem("dve_chain2")

        def rows(i):
            return P if i < NT else NS

        def limit(eng):
            return eng.value_load(njobs[0:1, 0:1], min_val=NE, max_val=NJ)

        def job_rows(eng, j):
            return eng.value_load(jobs[0:1, 2, bass.ds(j, 1)], min_val=0, max_val=CAP)

        block = ctx.enter_context(nc.Block())

        @block.sync
        def _(sp):
            sp.dma_start(l2g[:, :], o["ln2_g"].partition_broadcast(P)).then_inc(ln2_in, 16)
            sp.dma_start(l2b[:, :], o["ln2_b"].partition_broadcast(P)).then_inc(ln2_in, 16)

            def load_job(j, e):
                for c in range(4):
                    sp.wait_ge(up_done, FT * j - FT + 2 * c + 2)
                    load_chunk(sp, e, c)
                for c in range(2):
                    sp.wait_ge(down_done, 2 * j - 1 + c)
                    load_chunk(sp, e, 4 + c)

            with sp.Fori(1, NE) as j:
                load_job(j, j)
            last = limit(sp)
            with sp.Fori(NE, NJ) as j:
                with sp.If(j < last):
                    e = sp.value_load(jobs[0:1, 0, bass.ds(j, 1)], min_val=0, max_val=NE - 1)
                    load_job(j, e)
                with sp.Else():
                    sp.nop()
            sp.wait_ge(y_ready, NT + 1)
            sp.wait_ge(y_out, 16 * (NT + 1))

        @block.gpsimd
        def _(gp):
            nc.gpsimd.memset(xg[:, :, :], 0.0).then_inc(xg_zero, 1)

            def gather(j):
                gp.wait_ge(slots_ready, j + 1)
                gp.sem_inc(gathers, 1)
                for h in range(2):
                    nc.gpsimd.indirect_dma_start(
                        out=xg[:, h], out_offset=None, in_=x1_dram,
                        in_offset=bass.IndirectOffsetOnAxis(ap=idx_next[:, h:h + 1], axis=0),
                        bounds_check=R - 1, oob_is_err=False).then_inc(gathered[h], 16)

            def scatter(h, n):
                nc.gpsimd.indirect_dma_start(
                    out=acc_dram, out_offset=bass.IndirectOffsetOnAxis(ap=idx_cur[0:n, h:h + 1], axis=0),
                    in_=y[0:n, h], in_offset=None, compute_op=ALU.add).then_inc(scattered[h], 16)

            gp.wait_ge(xg_zero, 1)
            gather(0)
            gp.engine_nop().then_inc(y_free, 1)
            last = limit(gp)
            with gp.Fori(0, NJ) as j:
                with gp.If(j < last):
                    n = job_rows(gp, j)
                    gp.wait_ge(turned, j + 1)
                    gather(j + 1)
                    gp.wait_ge(ready, 1)
                    gp.wait_ge(y_read[0], j + 2)
                    gp.wait_ge(y_read[1], j + 2)
                    with gp.If(n > P):
                        scatter(1, P)
                    with gp.Else():
                        scatter(1, 2)
                    with gp.If(n > 96):
                        scatter(0, P)
                    with gp.Else():
                        with gp.If(n > FEW):
                            scatter(0, 96)
                        with gp.Else():
                            scatter(0, 64)
                    gp.wait_ge(scattered[0], 16 * j + 16)
                    gp.wait_ge(scattered[1], 16 * j + 16)
                    gp.sem_inc(y_free, 1)
                with gp.Else():
                    gp.nop()
            gp.wait_ge(gathered[0], 16 * last + 16)
            gp.wait_ge(gathered[1], 16 * last + 16)
            gp.sem_inc(gathers, 1)
            for i in range(NT + 1):
                m = rows(i)
                gp.dma_start(fin[0:m, i], acc_dram[i * P:i * P + m]).then_inc(acc_in[i], 16)
            for i in range(NT + 1):
                m = rows(i)
                gp.wait_ge(scaled2, i + 1)
                nc.gpsimd.tensor_tensor(fin[0:m, i], fin[0:m, i], l2b[0:m], ALU.add).then_inc(y_ready, 1)

        @block.tensor
        def _(pe):
            def slots(j):
                pe.wait_ge(onehot_ready, j + 1)
                for h in range(2):
                    for i in range(NT + 1):
                        mm = nc.tensor.matmul(px[0][:, 6 * h:6 * h + 6], onehot[0:rows(i), i, h * P:(h + 1) * P],
                                              pay[0:rows(i), i], start=i == 0, stop=i == NT)
                mm.then_inc(slots_done, 1)

            def turn(j, n, before=None):
                pe.wait_ge(gathered[0], 16 * j + 16)
                pe.wait_ge(gathered[1], 16 * j + 16)
                with pe.If(n > P):
                    if before is not None:
                        pe.wait_ge(y_read[0], before + 1)
                        pe.wait_ge(y_read[1], before + 1)
                    for k in range(KT):
                        nc.tensor.transpose(py[1][k // 4][:, (k % 4) * P:(k % 4 + 1) * P], xg[:, 1, k * P:(k + 1) * P],
                                            C("ident"))
                with pe.Else():
                    pe.nop()
                for k in range(KT):
                    mm = nc.tensor.transpose(px[k // 4][:, (k % 4) * P:(k % 4 + 1) * P], xg[:, 0, k * P:(k + 1) * P],
                                             C("ident"))
                mm.then_inc(turned, 1)

            def up(j, n):
                for f in range(FT):
                    c, q = divmod(f, 2)
                    if q == 0:
                        pe.wait_ge(chunk_in[c], 32 * j + 32)
                    w = ring[:, c].rearrange("p (k a n) -> p k a n", k=KT, a=2)
                    pe.wait_ge(pu_free, FT * j + f + 1)
                    for g in range(2):
                        for k in range(KT):
                            mm = nc.tensor.matmul(pu[f % 2][:, g, 0:n], w[:, k, g, q * P:(q + 1) * P], xgT[:, k, 0:n],
                                                  start=k == 0, stop=k == KT - 1)
                    mm.then_inc(up_done, 1)

            def down(j, n):
                for c in range(2):
                    pe.wait_ge(chunk_in[4 + c], 16 * j + 16)
                    pe.wait_ge(y_read[c], j + 1)
                    w = ring[:, 4 + c].rearrange("p (k n) -> p k n", k=FT)
                    if c == 0 and n > P:
                        pe.wait_ge(xgT_ready, j + 2)
                    for h in range((n + P - 1) // P):
                        m = min(P, n - h * P)
                        for k in range(FT):
                            if c == 0 and h == 0:
                                pe.wait_ge(hid_done, FT * j + k + 1)
                            mm = nc.tensor.matmul(py[h][c][0:m, :], hid[:, k, h * P:h * P + m], w[:, k],
                                                  start=k == 0, stop=k == FT - 1)
                    mm.then_inc(down_done, 1)

            def down_few(j):
                for c in range(2):
                    pe.wait_ge(chunk_in[4 + c], 16 * j + 16)
                    pe.wait_ge(y_read[c], j + 1)
                for k in range(FT):
                    pe.wait_ge(hid_done, FT * j + k + 1)
                    for c in range(2):
                        mm = nc.tensor.matmul(py[0][c][c * FEW:(c + 1) * FEW, :], hid[:, k, 0:FEW],
                                              ring[:, 4 + c, 512 * k:512 * (k + 1)], start=k == 0, stop=k == FT - 1)
                        if k == FT - 1:
                            mm.then_inc(down_done, 1)

            def by_rows(n, f, j):
                with pe.If(n > P):
                    with pe.If(n > 160):
                        f(j, 256)
                    with pe.Else():
                        f(j, 160)
                with pe.Else():
                    with pe.If(n > 96):
                        f(j, 128)
                    with pe.Else():
                        f(j, 96)

            pe.wait_ge(ready, 1)
            slots(0)
            turn(0, job_rows(pe, 0))
            last = limit(pe)
            with pe.Fori(0, NJ) as j:
                with pe.If(j < last):
                    n = job_rows(pe, j)
                    following = job_rows(pe, j + 1)
                    pe.wait_ge(xgT_ready, j + 1)
                    slots(j + 1)
                    by_rows(n, up, j)
                    turn(j + 1, following, j)
                    with pe.If(n > FEW):
                        by_rows(n, down, j)
                    with pe.Else():
                        down_few(j)
                with pe.Else():
                    pe.nop()

        @block.scalar
        def _(a):
            def copy_turned(j, n):
                with a.If(n > P):
                    a.wait_ge(turned, j + 1)
                    for q in range(2):
                        nc.scalar.activation(xgT[:, 4 * q:4 * q + 4, P:2 * P],
                                             py[1][q][:, :].rearrange("p (k s) -> p k s", k=4), ACT.Copy)
                with a.Else():
                    a.nop()
                a.wait_ge(turned, j + 1)
                for q in range(2):
                    ins = nc.scalar.activation(xgT[:, 4 * q:4 * q + 4, 0:P],
                                               px[q][:, :].rearrange("p (k s) -> p k s", k=4), ACT.Copy)
                ins.then_inc(xgT_ready, 1)

            copy_turned(0, job_rows(a, 0))
            last = limit(a)
            with a.Fori(0, NJ) as j:
                with a.If(j < last):
                    n = job_rows(a, j)
                    following = job_rows(a, j + 1)

                    def sigmoids(width):
                        for f in range(FT):
                            a.wait_ge(g_ready, FT * j + f + 1)
                            nc.scalar.activation(ss[:, f % 2, 0:width], gg[:, f % 2, 0:width], ACT.Sigmoid,
                                                 scale=SW_ALPHA).then_inc(sig_done, 1)
                    with a.If(n > P):
                        sigmoids(CAP)
                    with a.Else():
                        sigmoids(P)
                    copy_turned(j + 1, following)

                    def results_ready():
                        a.wait_ge(cur_ready, j + 1)
                        a.wait_ge(down_done, 2 * j + 1)
                    with a.If(n > P):
                        results_ready()
                        nc.scalar.activation(y[:, 1, 0:512], py[1][0][:, :], ACT.Copy, scale=gate_cur[:, 1:2])
                    with a.Else():
                        a.nop()
                    results_ready()
                    nc.scalar.activation(y[:, 0, 0:512], py[0][0][:, :], ACT.Copy, scale=gate_cur[:, 0:1]
                                         ).then_inc(y_read[0], 1)
                with a.Else():
                    a.nop()
            def ln2_root(i):
                a.wait_ge(var2, i + 1)
                nc.scalar.activation(mv2[0:rows(i), i, 3:4], mv2[0:rows(i), i, 1:2], ACT.Sqrt).then_inc(rstd2, 1)
            ln2_root(0)
            for i in range(NT + 1):
                m = rows(i)
                if i < NT:
                    ln2_root(i + 1)
                a.wait_ge(y_ready, i + 1)
                dst = o["y_prompt"][0, i * P:(i + 1) * P] if i < NT else o["y_sample"][:, 0]
                a.dma_start(dst, fin[0:m, i]).then_inc(y_out, 16)

        @block.vector
        def _(d):
            V = nc.vector
            ch = Chain(d, dve)
            for b in pu:
                V.memset(b[:, :, :], 0.0).then_inc(pu_free, 1)
            for h in range(2):
                for c in range(2):
                    ins = V.memset(py[h][c][:, :], 0.0)
                    if h == 1:
                        ins.then_inc(y_read[c], 1)
            ch.mark(V.memset(y[:, :, :], 0.0))
            ch.mark(V.tensor_scalar(binT[:, :, FT:], binT[:, :, FT:], 1.0, None, ALU.add))
            ch.mark(V.memset(pay[:, :, 0:1], 1.0))
            ch.mark(V.tensor_copy(pay[:, :, 1], C("part")))
            ch.mark(V.tensor_copy(pay[:, :, 2], C("tile0")))
            ch.mark(V.tensor_copy(gparts[:, :, :, 0], gates[:, :, :]))
            ch.wait()
            ch.do(V.tensor_tensor(grest[:, :, :], gates[:, :, :], gparts[:, :, :, 0], ALU.subtract))
            ch.do(V.tensor_copy(gparts[:, :, :, 1], grest[:, :, :]))
            ch.do(V.tensor_tensor(grest[:, :, :], grest[:, :, :], gparts[:, :, :, 1], ALU.subtract))
            ch.mark(V.tensor_copy(gparts[:, :, :, 2], grest[:, :, :]))
            ch.mark(V.tensor_copy(pads[:, :], C("pad")))

            def find_slots(j):
                e = d.value_load(jobs[0:1, 0, bass.ds(j, 1)], min_val=0, max_val=NE - 1)
                first = d.value_load(jobs[0:1, 1, bass.ds(j, 1)], min_val=0, max_val=TWICE)
                V.tensor_copy(pay[:, :, 3:6], gparts[:, :, bass.ds(e, 1)].rearrange("p i o c -> p i (o c)")
                              ).then_inc(dve, 1)
                V.tensor_tensor(onehot[:, :, :], rankm[:, :, bass.ds(e, 1)].broadcast_to([P, NT + 1, CAP]),
                                slot_rank[:, bass.ds(first, CAP)].unsqueeze(1).broadcast_to([P, NT + 1, CAP]),
                                ALU.is_equal).then_inc(onehot_ready, 1)

            def name_slots(j):
                d.wait_ge(slots_done, j + 1)
                got = px[0][:, 0:12].rearrange("p (h c) -> p h c", c=6)
                V.tensor_reduce(gate_next[:, :], got[:, :, 3:6], AX.X, ALU.add).then_inc(dve, 1)
                V.tensor_reduce(numbers[:, :], got[:, :, 1:3], AX.X, ALU.add).then_inc(dve, 1)
                V.scalar_tensor_tensor(pads[:, :], got[:, :, 0], -1.0, C("pad"), ALU.add, ALU.mult).then_inc(dve, 1)

            def number_slots(j):
                V.tensor_tensor(idx_next[:, :], pads[:, :], numbers[:, :], ALU.add).then_inc(slots_ready, 1)

            ch.wait()
            find_slots(0)
            ch.n += 1
            ch.wait()
            d.engine_nop().then_inc(ready, 1)
            name_slots(0)
            ch.n += 3
            ch.wait()
            number_slots(0)
            find_slots(1)
            ch.n += 1
            before = ch.n
            per_job = FT + 8
            last = limit(d)
            with d.Fori(0, NJ) as j:
                with d.If(j < last):
                    n = job_rows(d, j)
                    e = d.value_load(jobs[0:1, 0, bass.ds(j, 1)], min_val=0, max_val=NE - 1)

                    def hidden(width):
                        at = Chain(d, dve, before + per_job * j)
                        at.do(V.tensor_copy(jbias[:, :], binT[:, bass.ds(e, 1), :].rearrange("p o f -> p (o f)")))

                        def finish(f):
                            d.wait_ge(sig_done, FT * j + f + 1)
                            V.tensor_tensor(hid[:, f, 0:width], uu[:, f % 2, 0:width], ss[:, f % 2, 0:width], ALU.mult
                                            ).then_inc(hid_done, 1)

                        for f in range(FT):
                            d.wait_ge(up_done, FT * j + f + 1)
                            V.tensor_scalar(gg[:, f % 2, 0:width], pu[f % 2][:, 0, 0:width], jbias[:, f:f + 1], SW_LIMIT,
                                            ALU.add, ALU.min).then_inc(g_ready, 1)
                            V.tensor_scalar(uu[:, f % 2, 0:width], pu[f % 2][:, 1, 0:width],
                                            jbias[:, FT + f:FT + f + 1], SW_LIMIT + 1.0, ALU.add, ALU.min
                                            ).then_inc(pu_free, 1)
                            if f > 0:
                                finish(f - 1)
                            d.wait_ge(pu_free, FT * j + f + 3)
                            d.wait_ge(g_ready, FT * j + f + 1)
                            at.do(V.scalar_tensor_tensor(uu[:, f % 2, 0:width], uu[:, f % 2, 0:width], 1.0 - SW_LIMIT,
                                                         gg[:, f % 2, 0:width], ALU.max, ALU.mult))
                            if f == 0:
                                d.wait_ge(slots_ready, j + 1)
                                at.mark(V.tensor_copy(idx_held[:, :], idx_next[:, :]))
                                at.do(V.tensor_copy(gate_held[:, :], gate_next[:, :]))
                                name_slots(j + 1)
                                at.n += 3
                                at.wait()
                                number_slots(j + 1)
                            if f == 4:
                                find_slots(j + 2)
                                at.n += 1
                            if f == 6:
                                d.wait_ge(y_free, j + 1)
                                at.mark(V.tensor_copy(idx_cur[:, :], idx_held[:, :]))
                                V.tensor_copy(gate_cur[:, :], gate_held[:, :]).then_inc(cur_ready, 1)
                        finish(FT - 1)
                        return at.n

                    with d.If(n > P):
                        made = hidden(CAP)
                    with d.Else():
                        hidden(P)
                    assert made == per_job, made
                    def results_ready():
                        d.wait_ge(cur_ready, j + 1)
                        d.wait_ge(down_done, 2 * j + 2)
                    with d.If(n > P):
                        results_ready()
                        V.tensor_scalar(y[:, 1, 512:], py[1][1][:, :], gate_cur[:, 1:2], None, ALU.mult)
                    with d.Else():
                        d.nop()
                    with d.If(n > FEW):
                        results_ready()
                        V.tensor_scalar(y[:, 0, 512:], py[0][1][:, :], gate_cur[:, 0:1], None, ALU.mult
                                        ).then_inc(y_read[1], 1)
                    with d.Else():
                        results_ready()
                        V.tensor_scalar(y[0:FEW, 0, 512:], py[0][1][FEW:P, :], gate_cur[FEW:P, 0:1], None, ALU.mult
                                        ).then_inc(y_read[1], 1)
                with d.Else():
                    d.nop()
            fc = Chain(d, sem("ln2_chain"))
            d.wait_ge(ln2_in, 32)
            for i in range(NT + 1):
                m = rows(i)
                f = fin[0:m, i]
                d.wait_ge(acc_in[i], 16)
                for h in range(2):
                    fc.mark(V.bn_stats(bn2[0:m, h], f[:, h * 512:(h + 1) * 512]))
                fc.wait()
                fc.do(V.bn_aggr(mv2[0:m, i, 0:2], bn2[0:m].rearrange("p h s -> p (h s)")))
                V.tensor_scalar(mv2[0:m, i, 1:2], mv2[0:m, i, 1:2], EPS, None, ALU.add).then_inc(var2, 1)
                d.wait_ge(rstd2, i + 1)
                fc.do(V.reciprocal(mv2[0:m, i, 2:3], mv2[0:m, i, 3:4]))
                fc.do(V.tensor_scalar(f, f, mv2[0:m, i, 0:1], mv2[0:m, i, 2:3], ALU.subtract, ALU.mult))
                V.tensor_tensor(f, f, l2g[0:m], ALU.mult).then_inc(scaled2, 1)


_OUTS = [(1, SEQ, D), (NS, 1, D), (1, 1, PBUF, POOLW), (1, 1, CBUF, CONVW), (1, 1, SEQ, NH, HD), (1, 1, SEQ, NH, HD),
         (1, NS, PBUF, POOLW), (1, NS, CBUF, CONVW), (1, NS, 1, NH, HD), (1, NS, 1, NH, HD)]


def lay_out(inputs):
    g = {k: np.asarray(a) for k, a in inputs.items()}

    def tiles(a, n):
        return np.ascontiguousarray(np.swapaxes(a.reshape(n, P, *a.shape[1:]), 0, 1))

    x = np.concatenate([g["x_prompt"][0], g["x_sample"][:, 0]], 0)
    blocks = np.zeros((P, 2, P), np.float32)
    for i in range(2 * 2):
        lo = (i % 2) * HD
        blocks[lo:lo + HD, i // 2, lo:lo + HD] = g["pool_w"][0, i]
    per_channel = [tiles(g["conv_w"][0].T, 3).reshape(P, -1)] + [
        tiles(g[k][0], n) for k, n in (("conv_b", 3), ("conv_ln_g", 3), ("conv_ln_b", 3), ("pool_scale", 2))]
    return {
        "xT": tiles(x.T, KT),
        "x_prompt": g["x_prompt"], "x_sample": g["x_sample"],
        "pool_prefix": tiles(np.transpose(g["state_pool"][0], (2, 0, 1)), 2),
        "conv_prefix": tiles(np.transpose(g["state_conv"][0], (2, 0, 1)), 3),
        "state_pool": g["state_pool"], "state_conv": g["state_conv"],
        "cache_k": g["cache_attn_k"].reshape(NS, PAST, ATTW), "cache_v": g["cache_attn_v"].reshape(NS, PAST, ATTW),
        "w_in": g["w_in"], "pool_w": blocks, "chan": np.concatenate(per_channel, 1), "w_o": g["w_o"],
        "ln1_g": g["ln1_g"][0], "ln1_b": g["ln1_b"][0],
        "router_w": tiles(g["router_w"][0], KT), "router_b": g["router_b"],
        "e_in": g["expert_w_in"][0],
        "e_bin": np.ascontiguousarray(np.transpose(g["expert_b_in"][0].reshape(NE, 2 * FT, P), (2, 0, 1))),
        "e_out": g["expert_w_out"][0], "e_bout": g["expert_b_out"],
        "ln2_g": g["ln2_g"][0], "ln2_b": g["ln2_b"][0],
        "consts": constants(), "ranks": slot_ranks(), "pbias": prompt_bias(),
    }


def kernel(**inputs):
    import concourse.bacc as bacc
    from concourse.bass_utils import run_bass_kernel_spmd

    nc = bacc.Bacc("TRN2", target_bir_lowering=False, num_devices=1)
    arrays, args = {}, []
    for name, a in lay_out(inputs).items():
        a = np.ascontiguousarray(a)
        arrays[f"in_{name}"] = a
        args.append(nc.dram_tensor(f"in_{name}", a.shape, mybir.dt.from_np(a.dtype), kind="ExternalInput").ap())
    for i, shape in enumerate(_OUTS):
        args.append(nc.dram_tensor(f"out_{i}", shape, F32, kind="ExternalOutput").ap())
    layer(nc, *args)
    r = run_bass_kernel_spmd(nc, [arrays], core_ids=[0])
    return tuple(r.results[0][f"out_{i}"] for i in range(len(_OUTS)))
```

```python
import math
from contextlib import ExitStack

import numpy as np

import concourse.bass as bass
from concourse import mybir

F32 = mybir.dt.float32
BF16 = mybir.dt.bfloat16
F16 = mybir.dt.float16
I32 = mybir.dt.int32
U32 = mybir.dt.uint32
ALU = mybir.AluOpType
ACT = mybir.ActivationFunctionType
AX = mybir.AxisListType

P = 128
D = 1024
KT = D // P
SEQ = 512
NS = 8
R = SEQ + NS
HALF = R // 2
NT = SEQ // P
POOLW, ATTW, CONVW = 256, 384, 384
NH, HD = 6, 64
PROJ = POOLW + 3 * ATTW + 2 * CONVW
WINDOWS = (2, 4, 8, 16)
PBUF = max(WINDOWS) - 1
TAPS = 31
CBUF = TAPS - 1
PAST = 1024
DILATED = ((128, 1), (512, 4), (2048, 16))
NE, TOPK = 32, 4
FF = 1024
FT = FF // P
ALPHA_N = 2.0 ** 0.25
EPS = 1e-5
SW_ALPHA, SW_LIMIT = 1.702, 7.0
MASKED = -1e30

CAP = 2 * P
NOVER = 8
NJ = NE + NOVER
PAD0 = R
NROW = R + CAP
FEW = P // 2
TWICE = 3 * CAP

def _columns(widths):
    at, out = 0, {}
    for name, w in widths:
        out[name] = (at, at + w)
        at += w
    return out, at

CONST, NCONST = _columns([
    ("ident", P), ("tri", P), ("ones", P), ("mean", P), ("invw", 2), ("cnt", 2 * PBUF), ("wmask", 2 * PBUF),
    ("sel", NS * P), ("spread", NH * NS), ("headof", NH), ("sbias", 2 * P + 1), ("gather", NS),
    ("diag", NH * NS), ("pad", 2), ("part", NT + 1), ("tile0", NT + 1), ("exp", NE), ("jobno", NOVER)])
CHAN, NCHAN = _columns([("taps", 3 * TAPS), ("cb", 3), ("cg", 3), ("cbeta", 3), ("ps", 2)])


def slopes():
    def pow2(k):
        start = 2.0 ** (-8.0 / k)
        return [start ** (i + 1) for i in range(k)]
    c = 2 ** math.floor(math.log2(NH))
    return np.array(pow2(c) + pow2(2 * c)[0::2][:NH - c], np.float32)


def log_count(delta):
    n = sum(((delta >= 0) & (delta <= w) & (delta % d == 0)).astype(np.float64) for w, d in DILATED)
    return np.where(n > 0, np.log(np.maximum(n, 1)), MASKED)


def sample_rows():
    return np.concatenate([np.arange(PAST - P, PAST), np.arange(512, PAST - P, 4), np.arange(0, 512, 16)])


def constants():
    c = np.zeros((P, NCONST), np.float32)

    def put(name, a):
        lo, hi = CONST[name]
        a = np.asarray(a, np.float32)
        c[:a.shape[0], lo:hi] = a.reshape(a.shape[0], hi - lo)
    p = np.arange(P)
    put("ident", np.eye(P))
    put("tri", (p[:, None] < p[None, :]))
    put("ones", np.ones((P, P)))
    put("mean", np.full((P, P), 1.0 / CONVW))
    w = np.array([[WINDOWS[2 * i + (q // HD)] for i in range(2)] for q in range(P)])
    put("invw", 1.0 / w)
    t = np.arange(PBUF)
    put("cnt", 1.0 / np.minimum(w[:, :, None], t + 1))
    put("wmask", t[None, None, :] >= PBUF - (w[:, :, None] - 1))
    put("sel", np.repeat(np.eye(NS)[:, :, None], P, 2))
    b, h = np.divmod(np.arange(NS * NH), NH)
    put("spread", (b[None, :] == np.arange(NS)[:, None]))
    put("headof", (h[:, None] == np.arange(NH)))
    delta = np.append(PAST - sample_rows(), 0)
    put("sbias", log_count(delta) - slopes()[h][:, None] * delta)
    put("gather", b[:, None] == np.arange(NS))
    hb = np.arange(NH * NS)
    put("diag", (h[:, None] == hb // NS) & (b[:, None] == hb % NS))
    put("pad", -(PAD0 + p[:, None] + P * np.arange(2)))
    put("part", np.tile(p[:, None], (1, NT + 1)))
    put("tile0", np.tile(P * np.arange(NT + 1), (P, 1)))
    put("exp", np.tile(np.arange(NE), (P, 1)))
    put("jobno", np.tile(np.arange(NOVER), (P, 1)))
    return c


def slot_ranks():
    few, none = np.arange(FEW), np.full(CAP - 2 * FEW, 4 * CAP)
    a = np.concatenate([np.arange(TWICE), few, few, none, np.arange(P), P + few, P + few])
    return np.tile(a.astype(np.float16), (P, 1))


def prompt_bias():
    delta = np.arange(P)[:, None] + (NT - 1) * P - np.arange(SEQ)[None, :]
    b = log_count(delta)[:, None, :] - slopes()[None, :, None] * delta[:, None, :]
    return np.maximum(b, MASKED * 2).astype(np.float32)


STEPS = (["gate0", "a0", "gate1", "a1", "gate2", "a2", "pool0", "pool1", "states", "k0", "k1", "k2",
          "q0", "q1", "mean", "q2", "pw0", "var", "pw1", "ks", "qs", "v0", "kt0", "v1", "kt1", "v2", "kt2", "v3", "kt3", "v4"]
         + [f"qb{b}" for b in range(NS)] + ["pv0", "scored", "pv1", "pv2", "probs", "wo0", "wo1",
            "wo2", "bo0", "wo3", "bo1", "wo4", "bo2", "bo3", "bo4"])
SCORED_AT, SOFTMAX_AT = NS + 4, NS + 4
STEP = {name: i for i, name in enumerate(STEPS)}


class Chain:

    def __init__(self, eng, sem, base=0):
        self.eng, self.sem, self.base, self.n = eng, sem, base, 0

    def mark(self, ins):
        self.n += 1
        ins.then_inc(self.sem, 1)
        return self.n

    def wait(self, n=None):
        self.eng.wait_ge(self.sem, self.base + (self.n if n is None else n))

    def do(self, ins):
        self.mark(ins)
        self.wait()


def layer(nc, xT, x_prompt, x_sample, pool_prefix, conv_prefix, state_pool, state_conv, cache_k, cache_v,
          w_in, pool_w, chan, w_o, ln1_g, ln1_b, router_w, router_b, e_in, e_bin, e_brow, e_out, e_bout,
          ln2_g, ln2_b, consts, ranks, pbias,
          y_prompt, y_sample, p_pool, p_conv, p_k, p_v, s_pool, s_conv, s_k, s_v):
    x1_dram = nc.dram_tensor("x1_rows", [R, D], F32).ap()
    acc_dram = nc.dram_tensor("acc_rows", [NROW, D], F32).ap()

    with ExitStack() as outer:
        def keep(name, shape, dt=F32):
            return outer.enter_context(nc.sbuf_tensor(name, shape, dt))

        def sem(name):
            return outer.enter_context(nc.semaphore(name))

        ring = keep("ring", [P, 6, 4096])
        cst = keep("cst", [P, NCONST])
        slot_rank = keep("slot_rank", [P, TWICE + 2 * CAP], F16)
        rankm = keep("rankm", [P, NT + 1, NE])
        gates = keep("gates", [P, NT + 1, NE])
        jobs = keep("jobs", [1, 3, NJ + 3], I32)
        njobs = keep("njobs", [1, 1], I32)
        counts = keep("counts", [1, NE])
        binT = keep("binT", [P, NE, 2 * FT])

        def C(name, rows=P):
            lo, hi = CONST[name]
            return cst[0:rows, lo:hi]

        chunk_in = [sem(f"chunk_in{c}") for c in range(4)]
        out_in = [[sem(f"out_in_{name}{c}") for c in range(2)] for name in ("even", "odd")]

        def load_chunk(eng, e, c, out_room=ring[:, 4:6], odd=0):
            if c < 4:
                for g in range(2):
                    eng.dma_start(ring[:, c].rearrange("p (k a n) -> p k a n", k=KT, a=2)[:, :, g],
                                  e_in[bass.ds(e, 1), :, g * FF + 256 * c:g * FF + 256 * (c + 1)]
                                  .rearrange("o (k p) n -> p (o k) n", p=P)).then_inc(chunk_in[c], 16)
            else:
                eng.dma_start(out_room[:, c - 4].rearrange("p (k n) -> p k n", k=FT),
                              e_out[bass.ds(e, 1), :, 512 * (c - 4):512 * (c - 3)]
                              .rearrange("o (k p) n -> p (o k) n", p=P)).then_inc(out_in[odd][c - 4], 16)

        first_block(nc, locals())
        moe_block(nc, locals())



def first_block(nc, o):
    xT, x_prompt, x_sample, w_in, w_o, cache_k, cache_v, state_pool, state_conv = (
        o[k] for k in "xT x_prompt x_sample w_in w_o cache_k cache_v state_pool state_conv".split())
    ring, rankm, gates, jobs, njobs, counts, binT, C, load_chunk = (
        o[k] for k in "ring rankm gates jobs njobs counts binT C load_chunk".split())
    x1_dram, acc_dram = o["x1_dram"], o["acc_dram"]

    flat = ring[:, :, :].rearrange("p c n -> p (c n)")
    win = flat[:, 0:KT * PROJ]
    ATTN_IN = POOLW + 3 * ATTW

    def wcols(lo, hi):
        if lo >= ATTN_IN:
            return win[:, 0:KT * 2 * CONVW].rearrange("p (k n) -> p k n", k=KT)[:, :, lo - ATTN_IN:hi - ATTN_IN]
        return win[:, KT * 2 * CONVW:].rearrange("p (k n) -> p k n", k=KT)[:, :, lo:hi]
    pb = flat[:, 0:NH * SEQ].rearrange("p (h q) -> p h q", h=NH)
    sc0 = NH * SEQ
    sc = flat[:, sc0:sc0 + 2 * SEQ].rearrange("p (u q) -> p u q", u=2)
    pr = flat[:, sc0 + 2 * SEQ:sc0 + 5 * SEQ].rearrange("p (u q) -> p u q", u=3)
    pt0 = sc0 + 5 * SEQ
    assert pt0 <= KT * 2 * CONVW
    pt = flat[:, pt0:pt0 + 2 * NT * SEQ].rearrange("p (u j q) -> p u j q", u=2, j=NT)
    wo0 = pt0 + 2 * NT * SEQ
    wo = flat[:, wo0:wo0 + KT * D].rearrange("p (k n) -> p k n", k=KT)
    kc0 = 6 * 4096 - NS * 2 * ATTW
    assert wo0 + KT * D <= kc0 and KT * PROJ <= kc0
    kc = flat[:, kc0:].rearrange("p (b t f) -> p b t f", b=NS, t=2)
    vc = kc

    with ExitStack() as ctx:
        def sb(name, shape, dt=F32):
            return ctx.enter_context(nc.sbuf_tensor(name, shape, dt))

        def bsem(name):
            return ctx.enter_context(nc.semaphore(name))

        xt = sb("xt", [P, KT, R])
        late = xt[:, :, :].rearrange("p k r -> p (k r)")
        l1g, l1b = late[:, 0:D], late[:, D:2 * D]
        x1t = late[:, 2 * D:4 * D].rearrange("p (u k r) -> p u k r", u=2, k=KT)
        mix = sb("mix", [P, KT, R])
        scr = mix[:, 2:4, :]
        scr2 = mix[:, 4:6, :]
        prod = mix[:, 2:4, :].rearrange("p a r -> p (a r)")[:, 0:2 * ATTW].rearrange("p (t f) -> p t f", t=2)
        up = sb("up", [P, 2, PBUF + R])
        qT = sb("qT", [P, 3, R])
        kT = sb("kT", [P, 3, R])
        v = sb("v", [P, NT + 1, ATTW])
        conv = sb("conv", [P, 3 * R + 3 * (CBUF + R) + 3 * R])
        sig = conv[:, 0:3 * R].rearrange("p (i r) -> p i r", i=3)
        u = conv[:, 3 * R:6 * R + 3 * CBUF].rearrange("p (i r) -> p i r", i=3)
        cy = conv[:, 6 * R + 3 * CBUF:9 * R + 3 * CBUF].rearrange("p (i r) -> p i r", i=3)
        rst = u[:, 0, 0:R]
        x1 = conv[:, 0:2 * D].rearrange("p (u n) -> p u n", u=2)
        bout = conv[0:NE, 2 * D:3 * D]
        accs = [conv[:, 3 * D:4 * D], qT[:, :, :].rearrange("p i r -> p (i r)")[:, 0:D]]
        xtok = sb("xtok", [P, 2, D])
        ktok = xtok[:, 0, 0:2 * ATTW].rearrange("p (u f) -> p u f", u=2)
        ksam, qsam = xtok[0:NS, 1, 0:ATTW], xtok[0:NS, 1, ATTW:2 * ATTW]
        chan = sb("chan_sb", [P, NCHAN])
        pw = sb("pw", [P, 2, P])
        ppre = sb("ppre", [P, 2, NS, PBUF])
        cpre = sb("cpre", [P, 3, NS, CBUF])
        rw = sb("rw", [P, KT, NE])
        rb = sb("rb", [1, NE])
        st = sb("st", [NS + CBUF, POOLW + CONVW])
        ssc = sb("ssc", [P, 2, NH * NS])
        s48 = sb("s48", [NH * NS, 2 * P + 1])
        jr = s48[0:1, 3 * NE:7 * NE].rearrange("p (k e) -> p k e", e=NE)
        jf = s48[0:1, 7 * NE:7 * NE + 3 * (NOVER + 3)].rearrange("p (k j) -> p k j", k=3)
        jv = late[0:1, 2 * D:2 * D + 3 * NOVER * NE].rearrange("p (k v e) -> p k v e", k=3, e=NE)
        col48 = sb("col48", [NH * NS, 8])
        ps48 = sb("ps48", [P, 2, NH * NS])
        dg48 = sb("dg48", [NH * NS, NH * NS])
        dnew = sb("dnew", [NS, NH, NS])
        sn = sb("sn", [NS, NH])
        pool8 = sb("pool8", [P, 2, NS])
        conv8 = sb("conv8", [P, 3, NS])
        nsteps = NH * NT
        negm = sb("negm", [P, 4, nsteps])
        bn = sb("bn", [P, 2, 6])
        mv = sb("mv", [P, 4])
        lg = sb("lg", [P, NE])
        top = sb("top", [P, 8])
        topi = sb("topi", [P, 8], U32)
        tf = sb("tf", [P, 16])
        oh4 = sb("oh4", [P, TOPK, NE])
        og4 = sb("og4", [P, TOPK, NE])
        memb = sb("memb", [P, NT + 1, NE], BF16)
        trib = sb("tri_bf16", [P, 2, P], BF16)
        gT = sb("gT", [NE, P])
        zero = cpre[:, 0:2].rearrange("p i b t -> p (i b t)")[:, 0:D // 4]

        def chn(name):
            lo, hi = CHAN[name]
            return chan[:, lo:hi]
        taps = chn("taps").rearrange("p (i k) -> p i k", i=3)

        pair = [ctx.enter_context(nc.psum_tensor(f"pair{i}", [P, 2, 512], F32)) for i in range(2)]
        bS = [ctx.enter_context(nc.psum_tensor(f"bS{i}", [P, 512], F32)) for i in range(2)]
        bT = [ctx.enter_context(nc.psum_tensor(f"bT{i}", [P, 512], F32)) for i in range(2)]

        def bank(name):
            return pair[STEP[name] % 2]

        ld = {k: bsem(f"ld_{k}") for k in
              "xt gate0 a0 gate1 a1 gate2 a2 k q v pool cst ranks chan pw ppre cpre rw rb kc vc pb wo l1 xr0 xr1 bout bin"
              .split()}
        pe_step = bsem("pe_step")
        pair_free = [bsem(f"pair_free{i}") for i in range(2)]
        zeroed = bsem("zeroed")
        zero_made = bsem("zero_made")
        copied = bsem("state_copied")
        stored = bsem("stored")
        k_stored = [bsem(f"k_stored{i}") for i in range(2)]
        conv_done = bsem("conv_done")
        centered = bsem("centered")
        squared = bsem("squared")
        z_done = bsem("z_done")
        rst_done = bsem("rst_done")
        var_ready = bsem("ln1_var_ready")
        rstd_ready = bsem("ln1_rstd_ready")
        swish = bsem("swish")
        conv_out = bsem("conv_out")
        pool_d = bsem("pool_d")
        scored = bsem("sample_scored")
        sn_done = bsem("new_scored")
        s_exp = bsem("sample_exp")
        s_neg = bsem("sample_negmax")
        s_prob = bsem("sample_prob")
        qk_done = bsem("qk_done")
        s_max = bsem("row_max")
        exp_done = bsem("exp_done")
        s_recip = bsem("row_recip")
        normed = bsem("normed")
        tr_done = bsem("tr_done")
        pt_done = bsem("pt_done")
        pv_even = bsem("pv_even")
        x_scaled = bsem("x_scaled")
        x1_ready = bsem("x1_ready")
        x1_sent = [bsem(f"x1_sent{i}") for i in range(2)]
        acc_ready = bsem("acc_ready")
        acc_sent = [bsem(f"acc_sent{i}") for i in range(2)]
        pads_zeroed = bsem("pads_zeroed")
        sy_done = bsem("sample_values_done")
        sy_read = bsem("sample_values_read")
        SY0 = 2 * P
        bf_ready = bsem("bf16_constants_ready")
        x1T_done = bsem("x1T_done")
        x1T_ready = bsem("x1T_ready")
        lg_done = bsem("lg_done")
        top_neg = bsem("top_neg")
        top_exp = bsem("top_exp")
        g_ready = bsem("gates_ready")
        gT_done = bsem("gT_done")
        gT_ready = bsem("gT_ready")
        m_ready = bsem("members_ready")
        rank_done = bsem("rank_done")
        dve = bsem("dve_chain")
        act = bsem("act_chain")
        pool = bsem("pool_chain")

        def stepped(eng, name):
            eng.wait_ge(pe_step, STEP[name] + 1)

        def freed(name):
            return pair_free[STEP[name] % 2]

        def emptied(eng, name):
            eng.wait_ge(freed(name), STEP[name] // 2 + 1)

        def rows(i):
            return P if i < NT else NS

        def halves(ap):
            return ap.rearrange("p (h r) -> p h r", h=2)

        block = ctx.enter_context(nc.Block())

        @block.sync
        def _(sp):
            def proj_cols(name, lo, hi):
                sp.dma_start(wcols(lo, hi), w_in[0, :, lo:hi].rearrange("(k p) n -> p k n", p=P)
                             ).then_inc(ld[name], 16)
            c0 = POOLW + 3 * ATTW
            sp.dma_start(xt[:, 0:4], xT[:, 0:4]).then_inc(ld["xt"], 16)
            proj_cols("gate0", c0 + CONVW, c0 + CONVW + P)
            sp.dma_start(xt[:, 4:8], xT[:, 4:8]).then_inc(ld["xt"], 16)
            proj_cols("a0", c0, c0 + P)
            sp.dma_start(chan[:, :], o["chan"]).then_inc(ld["chan"], 16)
            for i in (1, 2):
                proj_cols(f"gate{i}", c0 + CONVW + i * P, c0 + CONVW + (i + 1) * P)
                proj_cols(f"a{i}", c0 + i * P, c0 + (i + 1) * P)
            proj_cols("pool", 0, POOLW)
            proj_cols("k", POOLW + ATTW, POOLW + 2 * ATTW)
            proj_cols("q", POOLW, POOLW + ATTW)
            proj_cols("v", POOLW + 2 * ATTW, POOLW + 3 * ATTW)
            for lo, hi, t, step in ((0, P, 0, 1), (0, 96, 1, 4), (96, P, 1, 16)):
                first = {1: PAST - P, 4: 512, 16: 0}[step]
                sp.dma_start(kc[lo:hi, :, t, :],
                             cache_k[:, first:first + step * (hi - lo):step, :].rearrange("b p f -> p b f")
                             ).then_inc(ld["kc"], 16)
            stepped(sp, "a2")
            sp.dma_start(pb, o["pbias"]).then_inc(ld["pb"], 16)
            emptied(sp, "states")
            keep_p, keep_c = PBUF, CBUF
            sp.dma_start(o["p_pool"][0, 0], st[0:keep_p, 0:POOLW]).then_inc(stored, 16)
            sp.dma_start(o["s_pool"][0, :, keep_p - 1], st[keep_p:keep_p + NS, 0:POOLW]).then_inc(stored, 16)
            sp.dma_start(o["p_conv"][0, 0], st[0:keep_c, POOLW:]).then_inc(stored, 16)
            sp.dma_start(o["s_conv"][0, :, keep_c - 1], st[keep_c:keep_c + NS, POOLW:]).then_inc(stored, 16)
            emptied(sp, "ks")
            sp.dma_start(o["s_k"][0, :, 0].rearrange("b h d -> b (h d)"), ksam).then_inc(k_stored[0], 16)

            def store_v(i):
                emptied(sp, f"v{i}")
                sp.dma_start(o["p_v"][0, 0, i * P:(i + 1) * P].rearrange("r h d -> r (h d)"), v[:, i]
                             ).then_inc(stored, 16)

            def store_k(i):
                emptied(sp, f"kt{i}")
                sp.dma_start(o["p_k"][0, 0, i * P:(i + 1) * P].rearrange("r h d -> r (h d)"), ktok[:, i % 2]
                             ).then_inc(k_stored[i % 2], 16)
            for i in range(NT):
                store_v(i)
                store_k(i)
            emptied(sp, f"v{NT}")
            sp.dma_start(o["s_v"][0, :, 0].rearrange("b h d -> b (h d)"), v[0:NS, NT]).then_inc(stored, 16)
            stepped(sp, f"v{NT}")
            sp.dma_start(wo, w_o[0].rearrange("(k p) n -> p k n", p=P)).then_inc(ld["wo"], 16)
            sp.dma_start(l1g, o["ln1_g"].partition_broadcast(P)).then_inc(ld["l1"], 16)
            sp.dma_start(l1b, o["ln1_b"].partition_broadcast(P)).then_inc(ld["l1"], 16)
            sp.wait_ge(scored, 1)
            for lo, hi, t, step in ((0, P, 0, 1), (0, 96, 1, 4), (96, P, 1, 16)):
                first = {1: PAST - P, 4: 512, 16: 0}[step]
                sp.dma_start(vc[lo:hi, :, t, :],
                             cache_v[:, first:first + step * (hi - lo):step, :].rearrange("b p f -> p b f")
                             ).then_inc(ld["vc"], 16)
            sp.wait_ge(conv_out, 1)
            sp.dma_start(bout, o["e_bout"][0]).then_inc(ld["bout"], 16)
            stepped(sp, "pv2")
            sp.wait_ge(exp_done, nsteps)
            sp.wait_ge(normed, nsteps)
            for c in (0, 1):
                load_chunk(sp, 0, c)
            stepped(sp, f"wo{NT}")
            for c in (2, 3, 4, 5):
                load_chunk(sp, 0, c)
            sp.wait_ge(stored, 16 * (NT + 1 + 4))
            sp.wait_ge(copied, 32)

        @block.gpsimd
        def _(gp):
            ch = Chain(gp, pool)
            nc.gpsimd.memset(u[:, :, 0:CBUF], 0.0).then_inc(zeroed, 1)
            nc.gpsimd.memset(up[:, :, 0:PBUF], 0.0).then_inc(zeroed, 1)
            nc.gpsimd.memset(memb[:, :, :], 0.0).then_inc(zeroed, 1)
            nc.gpsimd.memset(gates[:, :, :], 0.0).then_inc(zeroed, 1)
            def load_rows(i):
                src = x_prompt[0, i * P:(i + 1) * P] if i < NT else x_sample[:, 0]
                gp.dma_start(xtok[0:rows(i), i % 2], src).then_inc(ld[f"xr{i % 2}"], 16)

            for n in range(nsteps):
                gp.wait_ge(s_recip, n + 1)
                w = (n % NT + 1) * P
                if n == NS + 2:
                    gp.wait_ge(k_stored[0], 48)
                    gp.wait_ge(k_stored[1], 32)
                    gp.wait_ge(sn_done, 1)
                    load_rows(0)
                    load_rows(1)
                nc.gpsimd.tensor_scalar(pr[:, n % 3, 0:w], pr[:, n % 3, 0:w], negm[:, 3, n:n + 1], None, ALU.mult
                                        ).then_inc(normed, 1)
            gp.wait_ge(conv_out, 1)
            nc.gpsimd.memset(zero, 0.0).then_inc(zero_made, 1)
            gp.wait_ge(ld["l1"], 32)
            for i in range(NT):
                m = rows(i)
                gp.wait_ge(x_scaled, i + 1)
                if i < NT - 1:
                    load_rows(i + 2)
                nc.gpsimd.tensor_tensor(x1[0:m, i % 2], x1[0:m, i % 2], l1b[0:m], ALU.add).then_inc(x1_ready, 1)

        @block.scalar
        def _(a):
            def small_load(name, dst, src):
                a.dma_start(dst, src).then_inc(ld[name], 16)
            a.wait_ge(ld["xt"], 32)
            small_load("cst", o["cst"][:, :], o["consts"])
            small_load("ranks", o["slot_rank"][:, :], o["ranks"])
            small_load("ppre", ppre[:, :, :, :], o["pool_prefix"])
            small_load("cpre", cpre[:, :, :, :], o["conv_prefix"])
            small_load("pw", pw[:, :, :], o["pool_w"])
            small_load("rw", rw[:, :, :], o["router_w"])
            small_load("rb", rb[:, :], o["router_b"])
            small_load("bin", binT[:, :, :], o["e_bin"])
            a.dma_start(o["s_pool"][0, :, 0:PBUF - 1], state_pool[0, :, 1:PBUF]).then_inc(copied, 16)
            a.dma_start(o["s_conv"][0, :, 0:CBUF - 1], state_conv[0, :, 1:CBUF]).then_inc(copied, 16)

            def evac(name, dst, src, scale=1.0, func=ACT.Copy):
                stepped(a, name)
                nc.scalar.activation(dst, src, func, scale=scale).then_inc(freed(name), 1)

            for i in range(3):
                evac(f"gate{i}", halves(sig[:, i]), bank(f"gate{i}")[:, :, 0:HALF], func=ACT.Sigmoid)
            def evac_v(i):
                evac(f"v{i}", v[0:rows(i), i], bank(f"v{i}")[0:rows(i), 0, 0:ATTW])

            def evac_kt(i):
                if i >= 2:
                    a.wait_ge(k_stored[i % 2], 32 if i % 2 == 0 else 16)
                evac(f"kt{i}", ktok[:, i % 2], bank(f"kt{i}")[:, 0, 0:ATTW])

            for i in range(2):
                evac(f"pool{i}", halves(up[:, i, PBUF:]), bank(f"pool{i}")[:, :, 0:HALF])
            stepped(a, "states")
            nc.scalar.activation(st[0:PBUF + NS, 0:POOLW], bank("states")[0:PBUF + NS, 0, 0:POOLW], ACT.Copy
                                 ).then_inc(act, 1)
            evac("states", st[:, POOLW:], bank("states")[0:CBUF + NS, 1, 0:CONVW])
            for i in range(3):
                evac(f"k{i}", halves(kT[:, i]), bank(f"k{i}")[:, :, 0:HALF])
            for i in range(3):
                evac(f"q{i}", halves(qT[:, i]), bank(f"q{i}")[:, :, 0:HALF], scale=HD ** -0.5)
            evac("pw0", halves(mix[:, 0]), bank("pw0")[:, :, 0:HALF], scale=chn("ps")[:, 0:1])
            a.wait_ge(centered, 1)
            nc.scalar.activation(sig[:, :, :], cy[:, :, :], ACT.Square).then_inc(squared, 1)
            emptied(a, "var")
            nc.scalar.activation(rst, rst, ACT.Sqrt).then_inc(rst_done, 1)
            evac("pw1", halves(mix[:, 1]), bank("pw1")[:, :, 0:HALF], scale=chn("ps")[:, 1:2])
            evac("ks", ksam, bank("ks")[0:NS, 0, 0:ATTW])
            evac("qs", qsam, bank("qs")[0:NS, 0, 0:ATTW])
            for i in range(3):
                a.wait_ge(z_done, i + 1)
                nc.scalar.activation(sig[:, i], cy[:, i], ACT.Sigmoid, scale=chn("cg")[:, i:i + 1],
                                     bias=chn("cbeta")[:, i:i + 1]).then_inc(swish, 1)
            for i in range(NT):
                evac_v(i)
                evac_kt(i)
            evac_v(NT)
            for n in range(nsteps + 4):
                if n < nsteps:
                    w = (n % NT + 1) * P
                    a.wait_ge(s_max, n + 1)
                    if n >= 3:
                        a.wait_ge(tr_done, n - 2)
                    nc.scalar.activation(pr[:, n % 3, 0:w], sc[:, n % 2, 0:w], ACT.Exp,
                                         bias=negm[:, 1, n:n + 1], accum_out=negm[:, 2, n:n + 1]
                                         ).then_inc(exp_done, 1)
                if n == SOFTMAX_AT:
                    a.wait_ge(s_neg, 1)
                    nc.scalar.activation(s48[:, :], s48[:, :], ACT.Exp, bias=col48[:, 3:4], accum_out=col48[:, 4:5]
                                         ).then_inc(s_exp, 1)
                if n >= 4:
                    m = n - 4
                    h, i = divmod(m, NT)
                    a.wait_ge(tr_done, m + 1)
                    if h >= 2 and i == 0:
                        if h % 2 == 0:
                            a.wait_ge(pv_even, h // 2)
                        else:
                            stepped(a, f"pv{(h - 2) // 2}")
                    nc.scalar.activation(pt[:, h % 2, 0:i + 1, i * P:(i + 1) * P],
                                         bT[m % 2][:, 0:(i + 1) * P].rearrange("p (j q) -> p j q", q=P),
                                         ACT.Copy).then_inc(pt_done, 1)
                    if i == 2 and h % 2 == 0 and h >= 2:
                        hp = h // 2 - 1
                        a.wait_ge(sn_done, 1)
                        evac(f"pv{hp}", mix[:, 2 + hp, 0:SEQ], bank(f"pv{hp}")[:, 0])
            evac("pv2", mix[:, 4, 0:SEQ], bank("pv2")[:, 0])
            stepped(a, "probs")
            nc.scalar.activation(ps48[:, :, :], bank("probs")[:, 0, 0:2 * NH * NS].rearrange("p (t c) -> p t c", t=2),
                                 ACT.Copy).then_inc(act, 1)
            evac("probs", dnew[:, :, :], bank("probs")[0:NS, 1, 0:NH * NS].rearrange("p (h b) -> p h b", h=NH))
            def ln1_root(i):
                a.wait_ge(var_ready, i + 1)
                nc.scalar.activation(mv[0:rows(i), 3:4], mv[0:rows(i), 1:2], ACT.Sqrt).then_inc(rstd_ready, 1)
            ln1_root(0)
            ln1_root(1)
            a.wait_ge(zero_made, 1)
            for q in range(CAP // P):
                for c in range(4):
                    a.dma_start(acc_dram[PAD0 + q * P:PAD0 + (q + 1) * P, c * (D // 4):(c + 1) * (D // 4)], zero
                                ).then_inc(pads_zeroed, 16)

            def acc_store(i):
                a.wait_ge(acc_ready, i + 1)
                a.dma_start(acc_dram[i * P:i * P + rows(i)], accs[i % 2][0:rows(i)]
                            ).then_inc(acc_sent[i % 2], 16)

            def gates_turned(i):
                a.wait_ge(gT_done, i + 1)
                nc.scalar.activation(gT[:, 0:rows(i)], bS[1][0:NE, 0:rows(i)], ACT.Copy).then_inc(gT_ready, 1)

            for i in range(NT + 1):
                m = rows(i)
                a.wait_ge(x1_ready, i + 1)
                a.dma_start(x1_dram[i * P:i * P + m], x1[0:m, i % 2]).then_inc(x1_sent[i % 2], 16)
                for q in range(2):
                    a.wait_ge(x1T_done, 2 * i + q + 1)
                    nc.scalar.activation(x1t[:, i % 2, 4 * q:4 * q + 4, 0:m],
                                         bT[q][:, 0:4 * m].rearrange("p (k r) -> p k r", k=4), ACT.Copy
                                         ).then_inc(x1T_ready, 1)
                if i == 2:
                    a.wait_ge(sy_done, 3)
                    sy = bS[1][:, SY0:SY0 + 3 * 2 * NS].rearrange("p (g b j) -> p g b j", g=3, j=2)
                    nc.scalar.activation(mix[0:HD, 2:5, SEQ:R], sy[0:HD, :, :, 0], ACT.Copy).then_inc(act, 1)
                    nc.scalar.activation(mix[HD:P, 2:5, SEQ:R], sy[HD:P, :, :, 1], ACT.Copy).then_inc(sy_read, 1)
                if 1 <= i < NT:
                    ln1_root(i + 1)
                a.wait_ge(top_neg, i + 1)
                nc.scalar.activation(tf[0:m, 4:8], top[0:m, 0:4], ACT.Exp, bias=tf[0:m, 8:9],
                                     accum_out=tf[0:m, 9:10]).then_inc(top_exp, 1)
                if i < NT - 1:
                    gates_turned(i)
                    acc_store(i)
            gates_turned(NT - 1)
            gates_turned(NT)
            acc_store(NT - 1)
            acc_store(NT)
            a.wait_ge(acc_sent[0], 48)
            a.wait_ge(acc_sent[1], 32)
            a.wait_ge(pads_zeroed, 64 * (CAP // P))
            a.wait_ge(x1_sent[0], 48)
            a.wait_ge(x1_sent[1], 32)

        @block.tensor
        def _(pe):
            def begin(name):
                if STEP[name] >= 2:
                    pe.wait_ge(freed(name), STEP[name] // 2)
                return bank(name)

            def project(name, lo, waits):
                b = begin(name)
                for s in waits:
                    pe.wait_ge(*s)
                for h in range(2):
                    for k in range(KT):
                        mm = nc.tensor.matmul(b[:, h, 0:HALF], wcols(lo, lo + P)[:, k],
                                              xt[:, k, h * HALF:(h + 1) * HALF], start=k == 0, stop=k == KT - 1)
                mm.then_inc(pe_step, 1)

            c0 = POOLW + 3 * ATTW
            pe.wait_ge(ld["xt"], 32)
            for i in range(3):
                project(f"gate{i}", c0 + CONVW + i * P, [(ld[f"gate{i}"], 16)])
                project(f"a{i}", c0 + i * P, [(ld[f"a{i}"], 16)])
            for i in range(2):
                project(f"pool{i}", i * P, [(ld["pool"], 16)])
            pe.wait_ge(ld["cst"], 16)
            b = begin("states")
            emptied(pe, "pool1")
            emptied(pe, "a2")
            for f in range(2):
                nc.tensor.transpose(b[0:PBUF + NS, 0, f * P:(f + 1) * P], up[:, f, SEQ:PBUF + R], C("ident"))
            for f in range(3):
                mm = nc.tensor.transpose(b[0:CBUF + NS, 1, f * P:(f + 1) * P], u[:, f, SEQ:CBUF + R], C("ident"))
            mm.then_inc(pe_step, 1)
            for i in range(3):
                project(f"k{i}", POOLW + ATTW + i * P, [(ld["k"], 16)])

            def channel_sums(name, src, s):
                b = begin(name)
                pe.wait_ge(s, 1)
                for h in range(2):
                    for i in range(3):
                        mm = nc.tensor.matmul(b[:, h, 0:HALF], C("mean"), src[:, i, h * HALF:(h + 1) * HALF],
                                              start=i == 0, stop=i == 2)
                mm.then_inc(pe_step, 1)

            project("q0", POOLW, [(ld["q"], 16)])
            project("q1", POOLW + P, [])
            channel_sums("mean", cy, conv_done)
            project("q2", POOLW + 2 * P, [])
            pe.wait_ge(pool_d, 1)
            pe.wait_ge(ld["pw"], 16)

            def pool_product(i):
                b = begin(f"pw{i}")
                for h in range(2):
                    mm = nc.tensor.matmul(b[:, h, 0:HALF], pw[:, i], scr2[:, i, h * HALF:(h + 1) * HALF],
                                          start=True, stop=True)
                mm.then_inc(pe_step, 1)
            pool_product(0)
            channel_sums("var", sig, squared)
            pool_product(1)
            emptied(pe, "k2")
            emptied(pe, "q2")
            for name, src in (("ks", kT), ("qs", qT)):
                b = begin(name)
                for f in range(3):
                    mm = nc.tensor.transpose(b[0:NS, 0, f * P:(f + 1) * P], src[:, f, SEQ:R], C("ident"))
                mm.then_inc(pe_step, 1)
            pe.wait_ge(ld["v"], 16)

            def project_v(i):
                b = begin(f"v{i}")
                for k in range(KT):
                    mm = nc.tensor.matmul(b[0:rows(i), 0, 0:ATTW], xt[:, k, i * P:i * P + rows(i)],
                                          wcols(POOLW + 2 * ATTW, POOLW + 3 * ATTW)[:, k],
                                          start=k == 0, stop=k == KT - 1)
                mm.then_inc(pe_step, 1)

            def keys_row_major(i):
                b = begin(f"kt{i}")
                for f in range(3):
                    mm = nc.tensor.transpose(b[:, 0, f * P:(f + 1) * P], kT[:, f, i * P:(i + 1) * P], C("ident"))
                mm.then_inc(pe_step, 1)

            def spread_query(s):
                b = begin(f"qb{s}")
                nc.tensor.matmul(b[:, 0, 0:ATTW], C("sel", NS)[:, s * P:(s + 1) * P], qsam, start=True, stop=True
                                 ).then_inc(pe_step, 1)
            for i in range(NT):
                project_v(i)
                keys_row_major(i)
            project_v(NT)
            emptied(pe, "qs")
            emptied(pe, f"v{NT}")
            emptied(pe, "kt3")

            def sample_scored():
                b = begin("scored")
                pe.wait_ge(sn_done, 1)
                pe.wait_ge(scored, 1)
                nc.tensor.matmul(b[0:NH * NS, 0, 0:NH], C("spread", NS), sn[:, :], start=True, stop=True)
                for t in range(2):
                    mm = nc.tensor.transpose(b[0:NH * NS, 1, t * P:(t + 1) * P], ssc[:, t], C("ident"))
                mm.then_inc(pe_step, 1)

            def sample_probs():
                b = begin("probs")
                pe.wait_ge(s_prob, 2)
                for t in range(2):
                    nc.tensor.transpose(b[:, 0, t * NH * NS:(t + 1) * NH * NS], s48[:, t * P:(t + 1) * P],
                                        C("ident", NH * NS)[:, 0:NH * NS])
                nc.tensor.matmul(b[0:NS, 1, 0:NH * NS], C("gather", NH * NS), dg48[:, :], start=True, stop=True
                                 ).then_inc(pe_step, 1)

            def sample_values(g):
                if g == 0:
                    emptied(pe, "probs")
                    pe.wait_ge(ld["vc"], 48)
                sy = bS[1][:, SY0 + g * 2 * NS:SY0 + (g + 1) * 2 * NS].rearrange("p (b j) -> p b j", j=2)
                nc.tensor.matmul(sy, v[0:NS, NT, g * P:(g + 1) * P],
                                 dnew[:, 2 * g:2 * g + 2, :].rearrange("p j b -> p b j"), start=True, stop=False,
                                 skip_group_check=True)
                for s in range(NS):
                    for t in range(2):
                        mm = nc.tensor.matmul(sy[:, s], vc[:, s, t, g * P:(g + 1) * P],
                                              ps48[:, t, s * NH + 2 * g:s * NH + 2 * g + 2],
                                              start=False, stop=(s == NS - 1 and t == 1),
                                              skip_group_check=True)
                mm.then_inc(sy_done, 1)

            def scores(n):
                h, i = divmod(n, NT)
                lo = HD * (h % 2)
                if n >= 2:
                    pe.wait_ge(s_max, n - 1)
                nc.tensor.matmul(bS[n % 2][:, 0:(i + 1) * P], qT[lo:lo + HD, h // 2, i * P:(i + 1) * P],
                                 kT[lo:lo + HD, h // 2, 0:(i + 1) * P], start=True, stop=True
                                 ).then_inc(qk_done, 1)

            def turn(n):
                i = n % NT
                pe.wait_ge(normed, n + 1)
                if n >= 2:
                    pe.wait_ge(pt_done, n - 1)
                for j in range(i + 1):
                    mm = nc.tensor.transpose(bT[n % 2][:, j * P:(j + 1) * P], pr[:, n % 3, j * P:(j + 1) * P],
                                             C("ident"))
                mm.then_inc(tr_done, 1)

            def values(h):
                b = begin(f"pv{h // 2}") if h % 2 == 0 else bank(f"pv{h // 2}")
                lo = HD * (h % 2)
                pe.wait_ge(pt_done, NT * (h + 1))
                for j in range(NT):
                    mm = nc.tensor.matmul(b[lo:lo + HD, 0, j * P:SEQ], v[:, j, h * HD:(h + 1) * HD],
                                          pt[:, h % 2, j, j * P:SEQ], start=j == 0, stop=j == NT - 1)
                mm.then_inc(pe_step if h % 2 else pv_even, 1)

            for n in range(nsteps + 5):
                if n < nsteps:
                    scores(n)
                if n < NS:
                    spread_query(n)
                if 3 <= n < nsteps + 3:
                    turn(n - 3)
                if n >= 5 and (n - 5) % NT == NT - 1:
                    values((n - 5) // NT)
                if n == SCORED_AT:
                    sample_scored()
            sample_probs()

            def out_proj(i):
                b = begin(f"wo{i}")
                if i < NT:
                    for h in range(2):
                        for k in range(KT):
                            mm = nc.tensor.matmul(b[:, h], mix[:, k, i * P:(i + 1) * P],
                                                  wo[:, k, h * 512:(h + 1) * 512], start=k == 0, stop=k == KT - 1)
                else:
                    for k in range(KT):
                        for h in range(2):
                            mm = nc.tensor.matmul(b[h * FEW:h * FEW + NS, h], mix[:, k, SEQ:R],
                                                  wo[:, k, h * 512:(h + 1) * 512], start=k == 0, stop=k == KT - 1)
                mm.then_inc(pe_step, 1)

            def router(i):
                m = rows(i)
                pe.wait_ge(x1_ready, i + 1)
                for q in range(2):
                    if i >= 1:
                        pe.wait_ge(x1T_ready, 2 * i - 1 + q)
                    for k in range(4):
                        mm = nc.tensor.transpose(bT[q][:, k * m:(k + 1) * m], x1[0:m, i % 2, (4 * q + k) * P:(4 * q + k + 1) * P],
                                                 C("ident", m)[:, 0:m])
                    mm.then_inc(x1T_done, 1)
                if i < 3:
                    sample_values(i)
                if i >= 1:
                    pe.wait_ge(top_neg, i)
                nc.tensor.matmul(bS[0][0:m, 0:NE], C("ones", 1)[:, 0:m], rb[:, :], start=True, stop=False)
                for k in range(KT):
                    if k % 4 == 0:
                        pe.wait_ge(x1T_ready, 2 * i + k // 4 + 1)
                    mm = nc.tensor.matmul(bS[0][0:m, 0:NE], x1t[:, i % 2, k, 0:m], rw[:, k], start=False,
                                          stop=k == KT - 1)
                mm.then_inc(lg_done, 1)

            def expert_bias(i):
                m = rows(i)
                pe.wait_ge(g_ready, i + 1)
                if i >= 1:
                    pe.wait_ge(gT_ready, i)
                nc.tensor.transpose(bS[1][0:NE, 0:m], gates[0:m, i], C("ident", m)[:, 0:m]).then_inc(gT_done, 1)
                b = begin(f"bo{i}")
                pe.wait_ge(gT_ready, i + 1)
                for h in range(2):
                    mm = nc.tensor.matmul(b[0:m, h], gT[:, 0:m], bout[:, h * 512:(h + 1) * 512], start=True, stop=True)
                mm.then_inc(pe_step, 1)

            emptied(pe, "pw1")
            emptied(pe, "pv2")
            pe.wait_ge(conv_out, 1)
            pe.wait_ge(ld["wo"], 16)
            out_proj(0)
            out_proj(1)
            pe.wait_ge(ld["rw"], 16)
            pe.wait_ge(ld["rb"], 16)
            pe.wait_ge(ld["bout"], 16)
            for i in range(NT + 1):
                router(i)
                if i + 2 == NT:
                    pe.wait_ge(sy_read, 1)
                if i + 2 <= NT:
                    out_proj(i + 2)
                if i < NT - 1:
                    expert_bias(i)
            pe.wait_ge(m_ready, NT + 1)
            pe.wait_ge(bf_ready, 2)
            for i in range(NT + 1):
                for j in range(i + 1):
                    nc.tensor.matmul(bS[0][:, i * NE:(i + 1) * NE], trib[0:rows(j), 0 if j == i else 1],
                                     memb[0:rows(j), j], start=j == 0, stop=j == i)
            for j in range(NT + 1):
                mm = nc.tensor.matmul(bS[0][:, (NT + 1) * NE:(NT + 2) * NE], trib[0:rows(j), 1], memb[0:rows(j), j],
                                      start=j == 0, stop=j == NT)
            mm.then_inc(rank_done, 1)
            for i in (NT - 1, NT):
                expert_bias(i)

        @block.vector
        def _(d):
            V = nc.vector
            ch = Chain(d, dve)
            d.wait_ge(zeroed, 4)
            def glu(i):
                stepped(d, f"a{i}")
                emptied(d, f"gate{i}")
                V.tensor_tensor(halves(u[:, i, CBUF:]), bank(f"a{i}")[:, :, 0:HALF], halves(sig[:, i]), ALU.mult
                                ).then_inc(freed(f"a{i}"), 1)

            def conv_taps(i, lo, hi):
                for t in range(lo, hi):
                    ch.wait()
                    if t == 0:
                        ch.mark(V.tensor_scalar(cy[:, i, 0:SEQ], u[:, i, 0:SEQ], taps[:, i, 0:1], chn("cb")[:, i:i + 1],
                                                ALU.mult, ALU.add))
                    else:
                        ch.mark(V.scalar_tensor_tensor(cy[:, i, 0:SEQ], u[:, i, t:t + SEQ], taps[:, i, t:t + 1],
                                                       cy[:, i, 0:SEQ], ALU.mult, ALU.add))
            glu(0)
            emptied(d, "a0")
            d.wait_ge(ld["chan"], 16)
            conv_taps(0, 0, 16)
            glu(1)
            conv_taps(0, 16, TAPS)
            emptied(d, "a1")
            conv_taps(1, 0, 5)
            glu(2)
            conv_taps(1, 5, TAPS)
            emptied(d, "a2")
            conv_taps(2, 0, TAPS)
            d.wait_ge(ld["cpre"], 16)
            d.wait_ge(ld["ppre"], 16)
            d.wait_ge(ld["cst"], 16)
            d.wait_ge(ld["ranks"], 16)
            pre = sig[:, :, 0:NS * CBUF].rearrange("p i (b t) -> p i b t", b=NS)
            for i in range(3):
                ch.mark(V.tensor_tensor(pre[:, i], cpre[:, i], taps[:, i, 0:CBUF].unsqueeze(1).broadcast_to([P, NS, CBUF]),
                                        ALU.mult))
            ch.wait()
            ch.do(V.tensor_reduce(conv8[:, :, :], pre, AX.X, ALU.add))
            for i in range(3):
                ch.mark(V.scalar_tensor_tensor(conv8[:, i], u[:, i, CBUF + SEQ:], taps[:, i, CBUF:TAPS], conv8[:, i],
                                               ALU.mult, ALU.add))
            ch.wait()
            for i in range(3):
                ins = V.tensor_scalar(cy[:, i, SEQ:R], conv8[:, i], chn("cb")[:, i:i + 1], None, ALU.add)
                (ch.mark(ins) if i < 2 else ins.then_inc(conv_done, 1))
            emptied(d, "pool1")
            ch.do(V.tensor_tensor(scr[:, :, 0:SEQ], up[:, :, PBUF:PBUF + SEQ], up[:, :, PBUF - 1:PBUF - 1 + SEQ], ALU.add))
            def double(lo, i, src, dst, w):
                p = slice(lo, P)
                ch.mark(V.tensor_tensor(dst[p, i, w:SEQ], src[p, i, w:SEQ], src[p, i, 0:SEQ - w], ALU.add))
                ch.do(V.tensor_copy(dst[p, i, 0:w], src[p, i, 0:w]))
            double(HD, 0, scr, scr2, 2)
            ch.do(V.tensor_copy(scr2[0:HD, 0, 0:SEQ], scr[0:HD, 0, 0:SEQ]))
            double(0, 1, scr, scr2, 2)
            double(0, 1, scr2, scr, 4)
            ch.do(V.tensor_copy(scr2[0:HD, 1, 0:SEQ], scr[0:HD, 1, 0:SEQ]))
            double(HD, 1, scr, scr2, 8)
            cnt = C("cnt").rearrange("p (i t) -> p i t", i=2)
            ch.do(V.tensor_tensor(scr[:, :, 0:PBUF], scr2[:, :, 0:PBUF], cnt, ALU.mult))
            for i in range(2):
                ch.mark(V.scalar_tensor_tensor(scr2[:, i, PBUF:SEQ], scr2[:, i, PBUF:SEQ], C("invw")[:, i:i + 1],
                                               up[:, i, 2 * PBUF:PBUF + SEQ], ALU.mult, ALU.subtract))
            ch.mark(V.tensor_tensor(scr2[:, :, 0:PBUF], scr[:, :, 0:PBUF], up[:, :, PBUF:2 * PBUF], ALU.subtract))
            wm = C("wmask").rearrange("p (i t) -> p i t", i=2)
            pre = scr[:, :, 0:NS * PBUF].rearrange("p i (b t) -> p i b t", b=NS)
            ch.wait()
            for i in range(2):
                ch.mark(V.tensor_tensor(pre[:, i], ppre[:, i], wm[:, i].unsqueeze(1).broadcast_to([P, NS, PBUF]), ALU.mult))
            ch.wait()
            ch.do(V.tensor_reduce(pool8[:, :, :], pre, AX.X, ALU.add))
            ch.do(V.tensor_tensor(pool8[:, :, :], pool8[:, :, :], up[:, :, PBUF + SEQ:], ALU.add))
            for i in range(2):
                ins = V.scalar_tensor_tensor(scr2[:, i, SEQ:R], pool8[:, i], C("invw")[:, i:i + 1],
                                             up[:, i, PBUF + SEQ:], ALU.mult, ALU.subtract)
                (ch.mark(ins) if i == 0 else ins.then_inc(pool_d, 1))
            stepped(d, "mean")
            d.wait_ge(conv_done, 1)
            for i in range(3):
                ins = V.tensor_tensor(halves(cy[:, i]), halves(cy[:, i]), bank("mean")[:, :, 0:HALF], ALU.subtract)
                (ch.mark(ins) if i < 2 else ins.then_inc(freed("mean"), 1))
            emptied(d, "mean")
            ch.wait()
            d.engine_nop().then_inc(centered, 1)
            def sample_scores(s):
                stepped(d, f"qb{s}")
                if s == 0:
                    d.wait_ge(ld["kc"], 48)
                ins = V.tensor_tensor(prod, kc[:, s], bank(f"qb{s}")[:, 0, 0:ATTW].unsqueeze(1).broadcast_to([P, 2, ATTW]),
                                      ALU.mult)
                ins.then_inc(freed(f"qb{s}"), 1)
                emptied(d, f"qb{s}")
                return V.tensor_reduce(ssc[:, :, s * NH:(s + 1) * NH], prod.rearrange("p t (h e) -> p t h e", e=HD),
                                       AX.X, ALU.add)
            stepped(d, "var")
            V.tensor_scalar(halves(rst), bank("var")[:, :, 0:HALF], EPS, None, ALU.add).then_inc(freed("var"), 1)
            d.wait_ge(rst_done, 1)
            ch.do(V.reciprocal(rst, rst))
            for i in range(3):
                V.tensor_tensor(cy[:, i], cy[:, i], rst, ALU.mult).then_inc(z_done, 1)
            stepped(d, "pw1")
            for i in range(3):
                d.wait_ge(swish, i + 1)
                ch.mark(V.tensor_scalar(cy[:, i], cy[:, i], chn("cg")[:, i:i + 1], chn("cbeta")[:, i:i + 1],
                                        ALU.mult, ALU.add))
            ch.wait()
            for i in range(3):
                ins = V.tensor_tensor(mix[:, 5 + i], cy[:, i], sig[:, i], ALU.mult)
                (ch.mark(ins) if i < 2 else ins.then_inc(conv_out, 1))
            d.wait_ge(conv_out, 1)
            def new_key_scores():
                d.wait_ge(scored, 1)
                emptied(d, "ks")
                emptied(d, "qs")
                p8 = prod[0:NS, 0]
                ch.do(V.tensor_tensor(p8, qsam, ksam, ALU.mult))
                V.tensor_reduce(sn[:, :], p8.rearrange("p (h e) -> p h e", e=HD), AX.X, ALU.add).then_inc(sn_done, 1)

            def sample_max():
                stepped(d, "scored")
                ch.mark(V.tensor_tensor_reduce(dg48[:, 0:NH], bank("scored")[0:NH * NS, 0, 0:NH], C("headof", NH * NS),
                                               1.0, 0.0, ALU.mult, ALU.add, col48[:, 0:1]))
                V.tensor_tensor_reduce(s48[:, 0:2 * P], bank("scored")[0:NH * NS, 1, 0:2 * P],
                                       C("sbias", NH * NS)[:, 0:2 * P], 1.0, MASKED * 4, ALU.add, ALU.max,
                                       col48[:, 1:2]).then_inc(freed("scored"), 1)
                ch.wait()
                ch.do(V.tensor_tensor(s48[:, 2 * P:], col48[:, 0:1], C("sbias", NH * NS)[:, 2 * P:], ALU.add))
                emptied(d, "scored")
                ch.do(V.tensor_tensor(col48[:, 2:3], col48[:, 1:2], s48[:, 2 * P:], ALU.max))
                V.tensor_scalar(col48[:, 3:4], col48[:, 2:3], -1.0, None, ALU.mult).then_inc(s_neg, 1)

            def sample_normed():
                d.wait_ge(s_exp, 1)
                ch.do(V.reciprocal(col48[:, 5:6], col48[:, 4:5]))
                V.tensor_scalar(s48[:, :], s48[:, :], col48[:, 5:6], None, ALU.mult).then_inc(s_prob, 1)
                d.wait_ge(s_prob, 1)
                V.tensor_scalar(dg48[:, :], C("diag", NH * NS), s48[:, 2 * P:], None, ALU.mult).then_inc(s_prob, 1)

            d.wait_ge(ld["pb"], 16)
            for n in range(nsteps + 1):
                if n < NS:
                    ins = sample_scores(n)
                    ins.then_inc(scored, 1) if n == NS - 1 else ch.mark(ins)
                if n == NS:
                    new_key_scores()
                if n == SOFTMAX_AT:
                    sample_max()
                if n == SOFTMAX_AT + 1:
                    sample_normed()
                if n < nsteps:
                    h, i = divmod(n, NT)
                    w = (i + 1) * P
                    d.wait_ge(qk_done, n + 1)
                    if n >= 2:
                        d.wait_ge(exp_done, n - 1)
                    ch.do(V.tensor_tensor_reduce(sc[:, n % 2, 0:w], bS[n % 2][:, 0:w], pb[:, h, SEQ - w:SEQ], 1.0,
                                                 MASKED * 4, ALU.add, ALU.max, negm[:, 0, n:n + 1]))
                    V.tensor_scalar(negm[:, 1, n:n + 1], negm[:, 0, n:n + 1], -1.0, None, ALU.mult).then_inc(s_max, 1)
                if n >= 1:
                    d.wait_ge(exp_done, n)
                    V.reciprocal(negm[:, 3, n - 1:n], negm[:, 2, n - 1:n]).then_inc(s_recip, 1)
            def ln1(i):
                m = rows(i)
                stepped(d, f"wo{i}")
                d.wait_ge(ld[f"xr{i % 2}"], 16 * (i // 2 + 1))
                if i >= 2:
                    d.wait_ge(x1_sent[i % 2], 16 * (i // 2))
                    stepped(d, f"bo{i - 2}")
                xr = x1[0:m, i % 2]
                if i < NT:
                    V.scalar_tensor_tensor(xr, xtok[0:m, i % 2], ALPHA_N,
                                           bank(f"wo{i}")[0:m].rearrange("p h n -> p (h n)"), ALU.mult, ALU.add
                                           ).then_inc(freed(f"wo{i}"), 1)
                else:
                    b = bank(f"wo{i}")
                    V.tensor_scalar(xr[:, 512:], b[FEW:FEW + m, 1], 1.0, None, ALU.mult).then_inc(dve, 1)
                    ch.n += 1
                    ch.mark(V.scalar_tensor_tensor(xr[:, 0:512], xtok[0:m, i % 2, 0:512], ALPHA_N, b[0:m, 0],
                                                   ALU.mult, ALU.add))
                    ch.wait(ch.n - 1)
                    V.scalar_tensor_tensor(xr[:, 512:], xtok[0:m, i % 2, 512:], ALPHA_N, xr[:, 512:],
                                           ALU.mult, ALU.add).then_inc(freed(f"wo{i}"), 1)
                    ch.wait()
                emptied(d, f"wo{i}")
                for h in range(2):
                    ch.mark(V.bn_stats(bn[0:m, h], xr[:, h * 512:(h + 1) * 512]))
                ch.wait()
                ch.do(V.bn_aggr(mv[0:m, 0:2], bn[0:m].rearrange("p h s -> p (h s)")))
                V.tensor_scalar(mv[0:m, 1:2], mv[0:m, 1:2], EPS, None, ALU.add).then_inc(var_ready, 1)
                d.wait_ge(rstd_ready, i + 1)
                ch.do(V.reciprocal(mv[0:m, 2:3], mv[0:m, 3:4]))
                ch.do(V.tensor_scalar(xr, xr, mv[0:m, 0:1], mv[0:m, 2:3], ALU.subtract, ALU.mult))
                if i == 0:
                    d.wait_ge(ld["l1"], 32)
                if i < NT:
                    V.tensor_tensor(xr, xr, l1g[0:m], ALU.mult).then_inc(x_scaled, 1)
                else:
                    ch.do(V.tensor_tensor(xr, xr, l1g[0:m], ALU.mult))
                    V.tensor_tensor(xr, xr, l1b[0:m], ALU.add).then_inc(x1_ready, 1)

            def route(i):
                m = rows(i)
                d.wait_ge(lg_done, i + 1)
                ch.do(V.tensor_copy(lg[0:m], bS[0][0:m, 0:NE]))
                ch.do(V.max(top[0:m], lg[0:m]))
                V.tensor_scalar(tf[0:m, 8:9], top[0:m, 0:1], -1.0, None, ALU.mult).then_inc(top_neg, 1)
                ch.do(V.max_index(topi[0:m], top[0:m], lg[0:m]))
                ch.do(V.tensor_copy(tf[0:m, 0:4], topi[0:m, 0:4]))
                ch.do(V.tensor_tensor(oh4[0:m], C("exp", m).unsqueeze(1).broadcast_to([m, TOPK, NE]),
                                      tf[0:m, 0:4].unsqueeze(2).broadcast_to([m, TOPK, NE]), ALU.is_equal))
                with nc.allow_low_precision(reason="sums are 0 or 1"):
                    V.tensor_reduce(memb[0:m, i], oh4[0:m].rearrange("p k e -> p e k"), AX.X, ALU.add
                                    ).then_inc(m_ready, 1)
                d.wait_ge(top_exp, i + 1)
                ch.do(V.reciprocal(tf[0:m, 10:11], tf[0:m, 9:10]))
                ch.do(V.tensor_scalar(tf[0:m, 12:16], tf[0:m, 4:8], tf[0:m, 10:11], None, ALU.mult))
                ch.do(V.tensor_tensor(og4[0:m], oh4[0:m], tf[0:m, 12:16].unsqueeze(2).broadcast_to([m, TOPK, NE]),
                                      ALU.mult))
                V.tensor_reduce(gates[0:m, i], og4[0:m].rearrange("p k e -> p e k"), AX.X, ALU.add
                                ).then_inc(g_ready, 1)

            def acc_start(i):
                m = rows(i)
                stepped(d, f"bo{i}")
                if i >= 2:
                    d.wait_ge(acc_sent[i % 2], 16 * (i // 2))
                d.wait_ge(x1_ready, i + 1)
                V.scalar_tensor_tensor(accs[i % 2][0:m], x1[0:m, i % 2], ALPHA_N,
                                       bank(f"bo{i}")[0:m].rearrange("p h n -> p (h n)"), ALU.mult, ALU.add
                                       ).then_inc(freed(f"bo{i}"), 1)
                emptied(d, f"bo{i}")
                d.engine_nop().then_inc(acc_ready, 1)

            V.tensor_copy(trib[:, 0], C("tri")).then_inc(bf_ready, 1)
            V.tensor_copy(trib[:, 1], C("ones")).then_inc(bf_ready, 1)
            def job_table():
                OV, BASE, TMP, TMP2 = range(4)
                row = lambda k: jr[:, k, :]
                ch.mark(V.memset(jf, 0.0))
                ch.mark(V.tensor_scalar(row(OV), counts[:, :], float(CAP), None, ALU.is_gt))
                ch.do(V.tensor_scalar(row(TMP), counts[:, :], float(2 * CAP), None, ALU.is_gt))
                ch.do(V.tensor_tensor(row(OV), row(OV), row(TMP), ALU.add))
                ch.do(V.tensor_copy(row(TMP), row(OV)))
                a, b, w = TMP, TMP2, 1
                while w < NE:
                    ch.mark(V.tensor_copy(jr[:, b, 0:w], jr[:, a, 0:w]))
                    ch.do(V.tensor_tensor(jr[:, b, w:], jr[:, a, w:], jr[:, a, 0:NE - w], ALU.add))
                    a, b, w = b, a, 2 * w
                ch.mark(V.tensor_scalar(njobs[:, :], jr[:, a, NE - 1:], float(NE), None, ALU.add))
                ch.do(V.tensor_tensor(row(BASE), row(a), row(OV), ALU.subtract))
                over = lambda k: jv[:, k]
                both = lambda ap: ap.unsqueeze(1).broadcast_to([1, NOVER, NE])
                expert, first, number = (jf[:, k, 0:NOVER] for k in range(3))
                ch.do(V.tensor_tensor(over(0), C("jobno", 1).unsqueeze(2).broadcast_to([1, NOVER, NE]), both(row(BASE)),
                                      ALU.subtract))
                ch.mark(V.tensor_tensor(over(1), over(0), both(row(OV)), ALU.is_lt))
                ch.do(V.tensor_scalar(over(2), over(0), 0.0, None, ALU.is_ge))
                ch.do(V.tensor_tensor(over(1), over(1), over(2), ALU.mult))
                ch.do(V.tensor_tensor(over(2), over(1), both(C("exp", 1)), ALU.mult))
                ch.do(V.tensor_reduce(expert, over(2), AX.X, ALU.add))
                ch.do(V.tensor_scalar(over(0), over(0), 1.0, float(CAP), ALU.add, ALU.mult))
                ch.do(V.tensor_tensor(over(0), over(0), over(1), ALU.mult))
                ch.mark(V.tensor_reduce(first, over(0), AX.X, ALU.add))
                ch.do(V.tensor_tensor(over(2), over(1), both(counts[:, :]), ALU.mult))
                ch.do(V.tensor_reduce(number, over(2), AX.X, ALU.add))
                ch.do(V.tensor_tensor(number, number, first, ALU.subtract))
                ch.do(V.tensor_scalar(number, number, float(CAP), FEW + 1.0, ALU.min, ALU.max))
                gt, le = jv[:, 0, 0, 0:NOVER], jv[:, 0, 1, 0:NOVER]
                ch.mark(V.tensor_scalar(gt, number, float(P), float(FEW), ALU.is_gt, ALU.mult))
                ch.do(V.tensor_scalar(le, number, float(P + FEW), None, ALU.is_le))
                ch.do(V.tensor_tensor(gt, gt, le, ALU.mult))
                ch.do(V.tensor_tensor(number, number, gt, ALU.add))
                ch.mark(V.tensor_copy(jobs[:, :, NE:], jf))

            ln1(0)
            ln1(1)
            for i in range(NT + 1):
                route(i)
                if i < NT - 1:
                    acc_start(i)
                    ln1(i + 2)
            d.wait_ge(rank_done, 1)
            ch.do(V.tensor_scalar(rankm[:, :, :], memb[:, :, :], -1.0, 1e6, ALU.add, ALU.mult))
            ch.mark(V.tensor_tensor(rankm[:, :, :], rankm[:, :, :],
                                    bS[0][:, 0:(NT + 1) * NE].rearrange("p (i e) -> p i e", e=NE), ALU.add))
            ch.do(V.tensor_copy(counts[:, :], bS[0][0:1, (NT + 1) * NE:(NT + 2) * NE]))
            ch.mark(V.tensor_copy(jobs[:, 0, 0:NE], C("exp", 1)))
            few, many, tops = (s48[0:1, k * NE:(k + 1) * NE] for k in range(3))
            ch.mark(V.tensor_scalar(few, counts[:, :], float(FEW), float(TWICE), ALU.is_le, ALU.mult))
            ch.mark(V.tensor_scalar(many, counts[:, :], float(P), float(TWICE + CAP), ALU.is_gt, ALU.mult))
            ch.do(V.tensor_scalar(tops, counts[:, :], float(P + FEW), None, ALU.is_le))
            ch.do(V.tensor_tensor(many, many, tops, ALU.mult))
            ch.mark(V.tensor_tensor(jobs[:, 1, 0:NE], few, many, ALU.add))
            ch.mark(V.tensor_scalar(jobs[:, 2, 0:NE], counts[:, :], float(CAP), None, ALU.min))
            job_table()
            acc_start(NT - 1)
            acc_start(NT)
            ch.wait()


def moe_block(nc, o):
    ring, slot_rank, rankm, gates, jobs, njobs, counts, binT, C, sem, load_chunk, chunk_in, out_in = (
        o[k] for k in "ring slot_rank rankm gates jobs njobs counts binT C sem load_chunk chunk_in out_in".split())
    x1_dram, acc_dram = o["x1_dram"], o["acc_dram"]

    with ExitStack() as ctx:
        def sb(name, shape, dt=F32):
            return ctx.enter_context(nc.sbuf_tensor(name, shape, dt))

        def bsem(name):
            return ctx.enter_context(nc.semaphore(name))

        out_w = [ring[:, 4:6], sb("odd_out", [P, 2, 4096])[:, :]]
        xg = sb("xg", [P, 2, D])
        xgT = sb("xgT", [P, KT, CAP])
        hid = sb("hid", [P, FT, CAP])
        y = sb("y", [P, 2, D])
        gg = sb("gg", [P, 2, CAP])
        uu = sb("uu", [P, 2, CAP])
        ss = sb("ss", [P, 2, CAP])
        onehot = sb("onehot", [P, NT + 1, CAP], BF16)
        pay = sb("pay", [P, NT + 1, 6], BF16)
        gparts = sb("gparts", [P, NT + 1, NE, 3], BF16)
        grest = sb("grest", [P, NT + 1, NE])
        pads = sb("pads", [P, 2])
        numbers = sb("numbers", [P, 2])
        idx_next = sb("idx_next", [P, 2], I32)
        gate_next = sb("gate_next", [P, 2])
        idx_held = sb("idx_held", [P, 2], I32)
        gate_held = sb("gate_held", [P, 2])
        idx_run = sb("idx_run", [P, 2], I32)
        gate_run = sb("gate_run", [P, 2])
        raw = sb("raw", [P, 2, 6])
        idx_cur = sb("idx_cur", [P, 2], I32)
        gate_cur = sb("gate_cur", [P, 2])
        jbias = sb("jbias", [P, 2 * FT])
        brow = sb("brow", [NE, 4, 2, 256])
        chosen = sb("chosen", [NE, FEW])
        hrow = sb("hrow", [P, 2, 256])
        l2g = sb("l2g", [P, D])
        l2b = sb("l2b", [P, D])
        fin = out_w[1].rearrange("p c n -> p (c n)")[:, 0:(NT + 1) * D].rearrange("p (i n) -> p i n", n=D)
        bn2 = sb("bn2", [P, 2, 2, 6])
        mv2 = sb("mv2", [P, NT + 1, 5])

        pu = [ctx.enter_context(nc.psum_tensor(f"pu{i}", [P, 2, CAP], F32)) for i in range(2)]
        px = [ctx.enter_context(nc.psum_tensor(f"px{i}", [P, 512], F32)) for i in range(2)]
        py = [[ctx.enter_context(nc.psum_tensor(f"py{h}{c}", [P, 512], F32)) for c in range(2)] for h in range(2)]

        up_done = bsem("up_done")
        pu_free = bsem("pu_free")
        g_ready = bsem("gate_in_sbuf")
        sig_done = bsem("sigmoid_done")
        hid_done = bsem("hid_done")
        brow_in = bsem("brow_in")
        brow_ready = bsem("brow_ready")
        chosen_ready = bsem("chosen_ready")
        hid_turned = bsem("hid_turned")
        onehot_ready = bsem("onehot_ready")
        slots_done = bsem("slots_done")
        slots_read = bsem("slots_read")
        slots_ready = bsem("slots_ready")
        cur_ready = bsem("cur_ready")
        gathered = [bsem(f"gathered{h}") for h in range(2)]
        turned = bsem("turned")
        xgT_ready = bsem("xgT_ready")
        down_done = bsem("down_done")
        y_read = [bsem(f"y_read{c}") for c in range(2)]
        scattered = [bsem(f"scattered{h}") for h in range(2)]
        gathers = bsem("gathers")
        y_free = bsem("y_free")
        ready = bsem("results_zeroed")
        xg_zero = bsem("xg_zero")
        ln2_in = bsem("ln2_in")
        acc_in = [bsem(f"acc_in{i}") for i in range(NT + 1)]
        scaled2 = bsem("scaled2")
        sums_done = bsem("sums_done")
        shift2 = bsem("ln2_shift_ready")
        normed2 = bsem("ln2_normed")
        var2 = bsem("ln2_var_ready")
        rstd2 = bsem("ln2_rstd_ready")
        y_ready = bsem("y_ready")
        y_out = bsem("y_out")
        dve = bsem("dve_chain2")

        def rows(i):
            return P if i < NT else NS

        def load_sums(eng, i):
            eng.dma_start(fin[0:rows(i), i], acc_dram[i * P:i * P + rows(i)]).then_inc(acc_in[i], 16)

        def limit(eng):
            return eng.value_load(njobs[0:1, 0:1], min_val=NE, max_val=NJ)

        def job_rows(eng, j):
            return eng.value_load(jobs[0:1, 2, bass.ds(j, 1)], min_val=0, max_val=CAP)

        block = ctx.enter_context(nc.Block())

        @block.sync
        def _(sp):
            for a in range(2):
                sp.dma_start(brow[:, :, a], o["e_brow"][:, a * FF:(a + 1) * FF].rearrange("e (c n) -> e c n", n=256)
                             ).then_inc(brow_in, 16)

            def load_job(j, e, odd):
                for c in range(4):
                    sp.wait_ge(up_done, FT * j - FT + 2 * c + 2)
                    load_chunk(sp, e, c)
                for c in range(2):
                    sp.wait_ge(down_done, 2 * j - 3 + c)
                    load_chunk(sp, e, 4 + c, out_w[odd], odd)

            load_chunk(sp, 1, 4, out_w[1], 1)
            for h in range(2):
                sp.wait_ge(gathered[h], 16)
            load_chunk(sp, 1, 5, out_w[1], 1)
            for c in range(4):
                sp.wait_ge(up_done, 2 * c + 2)
                load_chunk(sp, 1, c)
            sp.dma_start(l2g[:, :], o["ln2_g"].partition_broadcast(P)).then_inc(ln2_in, 16)
            sp.dma_start(l2b[:, :], o["ln2_b"].partition_broadcast(P)).then_inc(ln2_in, 16)
            with sp.Fori(1, NE // 2) as two:
                for odd in range(2):
                    load_job(2 * two + odd, 2 * two + odd, odd)
            last = limit(sp)
            with sp.Fori(NE // 2, NJ // 2) as two:
                for odd in range(2):
                    with sp.If(2 * two + odd < last):
                        e = sp.value_load(jobs[0:1, 0, bass.ds(2 * two + odd, 1)], min_val=0, max_val=NE - 1)
                        load_job(2 * two + odd, e, odd)
                    with sp.Else():
                        sp.nop()
            sp.wait_ge(sums_done, 1)
            for i in (0, 2, 4):
                load_sums(sp, i)
            for i in range(NT + 1):
                sp.wait_ge(y_ready, i + 1)
                dst = o["y_prompt"][0, i * P:(i + 1) * P] if i < NT else o["y_sample"][:, 0]
                sp.dma_start(dst, fin[0:rows(i), i]).then_inc(y_out, 16)
            sp.wait_ge(y_out, 16 * (NT + 1))

        @block.gpsimd
        def _(gp):
            nc.gpsimd.memset(xg[:, :, :], 0.0).then_inc(xg_zero, 1)

            def by_quarters(n, f):
                with gp.If(n > 64):
                    with gp.If(n > 96):
                        f(128)
                    with gp.Else():
                        f(96)
                with gp.Else():
                    with gp.If(n > 32):
                        f(64)
                    with gp.Else():
                        f(32)

            def gather(j):
                n = job_rows(gp, j)
                gp.wait_ge(slots_ready, j + 1)
                gp.sem_inc(gathers, 1)

                def rows_of(h, m):
                    nc.gpsimd.indirect_dma_start(
                        out=xg[0:m, h], out_offset=None, in_=x1_dram,
                        in_offset=bass.IndirectOffsetOnAxis(ap=idx_next[0:m, h:h + 1], axis=0),
                        bounds_check=R - 1, oob_is_err=False).then_inc(gathered[h], 16)
                by_quarters(n, lambda m: rows_of(0, m))
                with gp.If(n > P):
                    rows_of(1, P)
                with gp.Else():
                    rows_of(1, 2)

            def scatter(h, n):
                nc.gpsimd.indirect_dma_start(
                    out=acc_dram, out_offset=bass.IndirectOffsetOnAxis(ap=idx_cur[0:n, h:h + 1], axis=0),
                    in_=y[0:n, h], in_offset=None, compute_op=ALU.add).then_inc(scattered[h], 16)

            gp.wait_ge(xg_zero, 1)
            gather(0)
            gp.wait_ge(turned, 1)
            gather(1)
            last = limit(gp)
            with gp.Fori(0, NJ) as j:
                with gp.If(j < last):
                    n = job_rows(gp, j)
                    gp.wait_ge(turned, j + 2)
                    gather(j + 2)
                    with gp.If(j > 0):
                        gp.wait_ge(scattered[0], 16 * j)
                        gp.wait_ge(scattered[1], 16 * j)
                        gp.sem_inc(y_free, 1)
                    with gp.Else():
                        gp.sem_inc(y_free, 1)
                    gp.wait_ge(ready, 1)
                    gp.wait_ge(y_read[0], j + 2)
                    gp.wait_ge(y_read[1], j + 2)
                    with gp.If(n > P):
                        with gp.If(n > P + FEW):
                            scatter(1, P)
                        with gp.Else():
                            scatter(1, FEW)
                    with gp.Else():
                        scatter(1, 2)
                    by_quarters(n, lambda m: scatter(0, m))
                with gp.Else():
                    gp.nop()
            for h in range(2):
                gp.wait_ge(gathered[h], 16 * last + 32)
                gp.wait_ge(scattered[h], 16 * last)
            gp.sem_inc(sums_done, 1)
            for i in range(NT + 1):
                m = rows(i)
                gp.wait_ge(scaled2, i + 1)
                nc.gpsimd.tensor_tensor(fin[0:m, i], fin[0:m, i], l2b[0:m], ALU.add).then_inc(y_ready, 1)

        @block.tensor
        def _(pe):
            def slots(j):
                pe.wait_ge(onehot_ready, j + 1)
                for h in range(2):
                    for i in range(NT + 1):
                        mm = nc.tensor.matmul(px[0][:, 6 * h:6 * h + 6], onehot[0:rows(i), i, h * P:(h + 1) * P],
                                              pay[0:rows(i), i], start=i == 0, stop=i == NT)
                mm.then_inc(slots_done, 1)

            def turn(j, n, before=None):
                pe.wait_ge(gathered[0], 16 * j + 16)
                pe.wait_ge(gathered[1], 16 * j + 16)
                pe.wait_ge(slots_read, j + 2)
                with pe.If(n > P):
                    for c in range(2):
                        pe.wait_ge(y_read[c], 1 if before is None else before + 1)
                    for k in range(KT):
                        nc.tensor.transpose(py[1][k // 4][:, (k % 4) * P:(k % 4 + 1) * P], xg[:, 1, k * P:(k + 1) * P],
                                            C("ident"))
                with pe.Else():
                    pe.nop()
                for k in range(KT):
                    mm = nc.tensor.transpose(px[k // 4][:, (k % 4) * P:(k % 4 + 1) * P], xg[:, 0, k * P:(k + 1) * P],
                                             C("ident"))
                mm.then_inc(turned, 1)

            def up(j, n):
                for f in range(FT):
                    c, q = divmod(f, 2)
                    if q == 0:
                        pe.wait_ge(chunk_in[c], 32 * j + 32)
                    w = ring[:, c].rearrange("p (k a n) -> p k a n", k=KT, a=2)
                    pe.wait_ge(pu_free, FT * j + f + 1)
                    for g in range(2):
                        for k in range(KT):
                            mm = nc.tensor.matmul(pu[f % 2][:, g, 0:n], w[:, k, g, q * P:(q + 1) * P], xgT[:, k, 0:n],
                                                  start=k == 0, stop=k == KT - 1)
                    mm.then_inc(up_done, 1)

            def up_few(j):
                pe.wait_ge(chosen_ready, j + 1)
                for q in range(2):
                    pe.wait_ge(chunk_in[2 * q], 32 * j + 32)
                    pe.wait_ge(chunk_in[2 * q + 1], 32 * j + 32)
                    pe.wait_ge(pu_free, FT * j + q + 1)
                    both = pu[q][:, :, :].rearrange("p g n -> p (g n)")
                    for c in range(2):
                        nc.tensor.matmul(both[c * FEW:(c + 1) * FEW], chosen[:, :],
                                         brow[:, 2 * q + c].rearrange("e a n -> e (a n)"), start=True, stop=False,
                                         skip_group_check=True)
                    for k in range(KT):
                        for c in range(2):
                            mm = nc.tensor.matmul(both[c * FEW:(c + 1) * FEW], xgT[:, k, 0:FEW],
                                                  ring[:, 2 * q + c, 512 * k:512 * (k + 1)], start=False,
                                                  stop=k == KT - 1, skip_group_check=True)
                    mm.then_inc(up_done, FT // 2)
                turn_hidden(j, 0)

            def turn_hidden(j, q):
                pe.wait_ge(hid_done, FT * j + FT // 2 * (q + 1))
                for t in range(2):
                    mm = nc.tensor.transpose(pu[q][:, 0, t * P:(t + 1) * P], hrow[:, q, t * P:(t + 1) * P], C("ident"))
                mm.then_inc(hid_turned, 1)

            def down_half(two, j, h, odd, first):
                for c in range(2):
                    if first:
                        pe.wait_ge(out_in[odd][c], 16 * two + 16)
                        pe.wait_ge(y_read[c], j + 1)
                    for k in range(FT):
                        if first and c == 0:
                            pe.wait_ge(hid_done, FT * j + k + 1)
                        mm = nc.tensor.matmul(py[h][c][:, :], hid[:, k, h * P:(h + 1) * P],
                                              out_w[odd][:, c, 512 * k:512 * (k + 1)], start=k == 0, stop=k == FT - 1)
                        if first and c == 0 and k == 0:
                            mm.then_inc(hid_turned, 2)
                    if h == 0:
                        mm.then_inc(down_done, 1)

            def down_few(two, j, h, odd, first):
                if first:
                    for c in range(2):
                        pe.wait_ge(out_in[odd][c], 16 * two + 16)
                        pe.wait_ge(y_read[c], j + 1)
                for k in range(FT):
                    if h == 1:
                        pe.wait_ge(hid_done, FT * j + k + 1)
                    elif k == 2:
                        turn_hidden(j, 1)
                    if h == 0 and k % 4 == 0:
                        pe.wait_ge(sig_done, FT * j + FT - 1 + k // 4)
                    for c in range(2):
                        mm = nc.tensor.matmul(py[h][c][c * FEW:(c + 1) * FEW, :], hid[:, k, h * P:h * P + FEW],
                                              out_w[odd][:, c, 512 * k:512 * (k + 1)], start=k == 0, stop=k == FT - 1)
                        if h == 0 and k == FT - 1:
                            mm.then_inc(down_done, 1)
                        if h == 1 and k == 0 and c == 0:
                            mm.then_inc(hid_turned, 2)

            def run_up(j, n):
                with pe.If(n > P):
                    with pe.If(n > 160):
                        up(j, 256)
                    with pe.Else():
                        up(j, 160)
                with pe.Else():
                    with pe.If(n > FEW):
                        up(j, 128)
                    with pe.Else():
                        up_few(j)

            def run_down(two, j, n, odd):
                with pe.If(n > P):
                    pe.wait_ge(xgT_ready, j + 2)
                    with pe.If(n > P + FEW):
                        down_half(two, j, 1, odd, True)
                    with pe.Else():
                        down_few(two, j, 1, odd, True)
                    down_half(two, j, 0, odd, False)
                with pe.Else():
                    with pe.If(n > FEW):
                        down_half(two, j, 0, odd, True)
                    with pe.Else():
                        down_few(two, j, 0, odd, True)

            slots(0)
            pe.wait_ge(slots_read, 1)
            slots(1)
            turn(0, job_rows(pe, 0))
            pe.wait_ge(brow_ready, 1)
            last = limit(pe)
            def job(two, odd):
                j = 2 * two + odd
                with pe.If(j < last):
                    n = job_rows(pe, j)
                    following = job_rows(pe, j + 1)
                    pe.wait_ge(xgT_ready, j + 1)
                    slots(j + 2)
                    run_up(j, n)
                    turn(j + 1, following, j)
                    run_down(two, j, n, odd)
                with pe.Else():
                    pe.nop()

            with pe.Fori(0, NJ // 2) as two:
                job(two, 0)
                job(two, 1)

        @block.scalar
        def _(a):
            def copy_turned(j, n):
                with a.If(n > P):
                    a.wait_ge(turned, j + 1)
                    for q in range(2):
                        nc.scalar.activation(xgT[:, 4 * q:4 * q + 4, P:2 * P],
                                             py[1][q][:, :].rearrange("p (k s) -> p k s", k=4), ACT.Copy)
                with a.Else():
                    a.nop()
                a.wait_ge(turned, j + 1)
                for q in range(2):
                    ins = nc.scalar.activation(xgT[:, 4 * q:4 * q + 4, 0:P],
                                               px[q][:, :].rearrange("p (k s) -> p k s", k=4), ACT.Copy)
                ins.then_inc(xgT_ready, 1)

            copy_turned(0, job_rows(a, 0))
            last = limit(a)
            with a.Fori(0, NJ) as j:
                with a.If(j < last):
                    n = job_rows(a, j)
                    following = job_rows(a, j + 1)

                    def sigmoids(width):
                        for f in range(FT):
                            a.wait_ge(g_ready, FT * j + f + 1)
                            nc.scalar.activation(ss[:, f % 2, 0:width], gg[:, f % 2, 0:width], ACT.Sigmoid,
                                                 scale=SW_ALPHA).then_inc(sig_done, 1)

                    def copy_hidden(q):
                        a.wait_ge(hid_turned, 2 * j + q + 1)
                        nc.scalar.activation(hid[:, 4 * q:4 * q + 4, 0:FEW].rearrange("p (g t) s -> p g t s", g=2),
                                             pu[q][:, 0, :].rearrange("p (t g s) -> p g t s", t=2, g=2), ACT.Copy
                                             ).then_inc(sig_done, 1)
                    with a.If(n > P):
                        sigmoids(CAP)
                    with a.Else():
                        with a.If(n > FEW):
                            sigmoids(P)
                        with a.Else():
                            for q in range(2):
                                a.wait_ge(g_ready, FT * j + FT // 2 * (q + 1))
                                nc.scalar.activation(ss[:, q, :], gg[:, q, :], ACT.Sigmoid, scale=SW_ALPHA
                                                     ).then_inc(sig_done, FT // 2 - 1)
                            copy_hidden(0)
                    copy_turned(j + 1, following)
                    with a.If(n > FEW):
                        a.nop()
                    with a.Else():
                        copy_hidden(1)

                    def results_ready():
                        a.wait_ge(cur_ready, j + 1)
                        a.wait_ge(down_done, 2 * j + 1)
                    with a.If(n > P):
                        results_ready()
                        nc.scalar.activation(y[:, 1, 0:512], py[1][0][:, :], ACT.Copy, scale=gate_cur[:, 1:2])
                    with a.Else():
                        a.nop()
                    results_ready()
                    nc.scalar.activation(y[:, 0, 0:512], py[0][0][:, :], ACT.Copy, scale=gate_cur[:, 0:1]
                                         ).then_inc(y_read[0], 1)
                with a.Else():
                    a.nop()
            def ln2_root(i):
                a.wait_ge(var2, i + 1)
                nc.scalar.activation(mv2[0:rows(i), i, 3:4], mv2[0:rows(i), i, 1:2], ACT.Sqrt).then_inc(rstd2, 1)
            a.wait_ge(sums_done, 1)
            for i in (1, 3):
                load_sums(a, i)
            for i in range(NT + 2):
                if i <= NT:
                    ln2_root(i)
                if i >= 1:
                    m = rows(i - 1)
                    a.wait_ge(shift2, i)
                    nc.scalar.activation(fin[0:m, i - 1], fin[0:m, i - 1], ACT.Identity, bias=mv2[0:m, i - 1, 4:5],
                                         scale=mv2[0:m, i - 1, 2:3]).then_inc(normed2, 1)

        @block.vector
        def _(d):
            V = nc.vector
            ch = Chain(d, dve)
            def find_slots(j):
                e = d.value_load(jobs[0:1, 0, bass.ds(j, 1)], min_val=0, max_val=NE - 1)
                first = d.value_load(jobs[0:1, 1, bass.ds(j, 1)], min_val=0, max_val=TWICE + CAP)
                V.tensor_copy(pay[:, :, 3:6], gparts[:, :, bass.ds(e, 1)].rearrange("p i o c -> p i (o c)")
                              ).then_inc(dve, 1)
                V.tensor_tensor(onehot[:, :, :], rankm[:, :, bass.ds(e, 1)].broadcast_to([P, NT + 1, CAP]),
                                slot_rank[:, bass.ds(first, CAP)].unsqueeze(1).broadcast_to([P, NT + 1, CAP]),
                                ALU.is_equal).then_inc(onehot_ready, 1)

            def choose(j):
                e = d.value_load(jobs[0:1, 0, bass.ds(j, 1)], min_val=0, max_val=NE - 1)
                V.tensor_copy(chosen[:, :], C("ident", NE)[:, bass.ds(e, 1)].broadcast_to([NE, FEW])
                              ).then_inc(chosen_ready, 1)

            def read_slots(j):
                d.wait_ge(slots_done, j + 1)
                V.tensor_copy(raw[:, :, :], px[0][:, 0:12].rearrange("p (h c) -> p h c", c=6)).then_inc(slots_read, 1)

            def name_slots(at, j):
                d.wait_ge(slots_read, j + 1)
                at.mark(V.tensor_reduce(gate_next[:, :], raw[:, :, 3:6], AX.X, ALU.add))
                at.mark(V.tensor_reduce(numbers[:, :], raw[:, :, 1:3], AX.X, ALU.add))
                at.do(V.scalar_tensor_tensor(pads[:, :], raw[:, :, 0], -1.0, C("pad"), ALU.add, ALU.mult))
                V.tensor_tensor(idx_next[:, :], pads[:, :], numbers[:, :], ALU.add).then_inc(slots_ready, 1)

            def hold_slots(at, j):
                for h in range(2):
                    d.wait_ge(gathered[h], 16 * j + 16)
                d.wait_ge(slots_ready, j + 1)
                at.mark(V.tensor_copy(idx_held[:, :], idx_next[:, :]))
                at.do(V.tensor_copy(gate_held[:, :], gate_next[:, :]))
                name_slots(at, j + 1)

            ch.mark(V.memset(pay[:, :, 0:1], 1.0))
            ch.mark(V.tensor_copy(pay[:, :, 1], C("part")))
            ch.mark(V.tensor_copy(pay[:, :, 2], C("tile0")))
            ch.do(V.tensor_copy(gparts[:, :, :, 0], gates[:, :, :]))
            ch.do(V.tensor_tensor(grest[:, :, :], gates[:, :, :], gparts[:, :, :, 0], ALU.subtract))
            ch.do(V.tensor_copy(gparts[:, :, :, 1], grest[:, :, :]))
            ch.do(V.tensor_tensor(grest[:, :, :], grest[:, :, :], gparts[:, :, :, 1], ALU.subtract))
            ch.do(V.tensor_copy(gparts[:, :, :, 2], grest[:, :, :]))
            find_slots(0)
            ch.n += 1
            choose(0)
            ch.mark(V.tensor_scalar(binT[:, :, FT:], binT[:, :, FT:], 1.0, None, ALU.add))
            ch.wait()
            read_slots(0)
            name_slots(ch, 0)
            find_slots(1)
            ch.n += 1
            read_slots(1)
            for b in pu:
                V.memset(b[:, :, :], 0.0).then_inc(pu_free, 1)
            for h in range(2):
                for c in range(2):
                    ins = V.memset(py[h][c][:, :], 0.0)
                    if h == 1:
                        ins.then_inc(y_read[c], 1)
            d.wait_ge(brow_in, 32)
            V.tensor_scalar(brow[:, :, 1], brow[:, :, 1], 1.0, None, ALU.add).then_inc(brow_ready, 1)
            find_slots(2)
            ch.n += 1
            hold_slots(ch, 0)
            V.memset(y[:, :, :], 0.0).then_inc(ready, 1)
            before = ch.n
            per_job = FT + 10
            last = limit(d)
            with d.Fori(0, NJ) as j:
                with d.If(j < last):
                    n = job_rows(d, j)
                    e = d.value_load(jobs[0:1, 0, bass.ds(j, 1)], min_val=0, max_val=NE - 1)

                    def hidden(width):
                        at = Chain(d, dve, before + per_job * j)
                        at.do(V.tensor_copy(jbias[:, :], binT[:, bass.ds(e, 1), :].rearrange("p o f -> p (o f)")))

                        def finish(f):
                            d.wait_ge(sig_done, FT * j + f + 1)
                            V.tensor_tensor(hid[:, f, 0:width], uu[:, f % 2, 0:width], ss[:, f % 2, 0:width], ALU.mult
                                            ).then_inc(hid_done, 1)

                        for f in range(FT):
                            d.wait_ge(up_done, FT * j + f + 1)
                            V.tensor_scalar(gg[:, f % 2, 0:width], pu[f % 2][:, 0, 0:width], jbias[:, f:f + 1], SW_LIMIT,
                                            ALU.add, ALU.min).then_inc(g_ready, 1)
                            V.tensor_scalar(uu[:, f % 2, 0:width], pu[f % 2][:, 1, 0:width],
                                            jbias[:, FT + f:FT + f + 1], SW_LIMIT + 1.0, ALU.add, ALU.min
                                            ).then_inc(pu_free, 1)
                            if f > 0:
                                finish(f - 1)
                            d.wait_ge(pu_free, FT * j + f + 3)
                            d.wait_ge(g_ready, FT * j + f + 1)
                            at.do(V.scalar_tensor_tensor(uu[:, f % 2, 0:width], uu[:, f % 2, 0:width], 1.0 - SW_LIMIT,
                                                         gg[:, f % 2, 0:width], ALU.max, ALU.mult))
                            if f == 0:
                                start(at)
                            if f == 4:
                                find_slots(j + 3)
                                at.n += 1
                            if f == 6:
                                hold_slots(at, j + 1)
                        finish(FT - 1)
                        choose(j + 1)
                        take_slots(at, 1)
                        return at.n

                    def start(at):
                        read_slots(j + 2)
                        at.mark(V.tensor_copy(idx_run[:, :], idx_held[:, :]))
                        at.do(V.tensor_copy(gate_run[:, :], gate_held[:, :]))

                    def take_slots(at, count):
                        d.wait_ge(y_free, j + 1)
                        V.tensor_copy(idx_cur[:, :], idx_run[:, :]).then_inc(dve, count)
                        at.n += count
                        V.tensor_copy(gate_cur[:, :], gate_run[:, :]).then_inc(cur_ready, 1)

                    def hidden_few():
                        at = Chain(d, dve, before + per_job * j)
                        start(at)
                        for q in range(2):
                            part = FT // 2 * (q + 1)
                            d.wait_ge(up_done, FT * j + part)
                            V.tensor_scalar(gg[:, q, :], pu[q][:, 0, :], SW_LIMIT, None, ALU.min
                                            ).then_inc(g_ready, FT // 2)
                            V.tensor_scalar(uu[:, q, :], pu[q][:, 1, :], SW_LIMIT + 1.0, None, ALU.min
                                            ).then_inc(pu_free, FT // 2)
                            d.wait_ge(pu_free, FT * j + part + 2)
                            d.wait_ge(g_ready, FT * j + part)
                            at.do(V.scalar_tensor_tensor(uu[:, q, :], uu[:, q, :], 1.0 - SW_LIMIT, gg[:, q, :],
                                                         ALU.max, ALU.mult))
                            d.wait_ge(sig_done, FT * j + (FT // 2 - 1) * (q + 1))
                            V.tensor_tensor(hrow[:, q, :], uu[:, q, :], ss[:, q, :], ALU.mult
                                            ).then_inc(hid_done, FT // 2)
                            if q == 0:
                                find_slots(j + 3)
                                at.n += 1
                        hold_slots(at, j + 1)
                        choose(j + 1)
                        take_slots(at, per_job - at.n)

                    with d.If(n > P):
                        made = hidden(CAP)
                    with d.Else():
                        with d.If(n > FEW):
                            hidden(P)
                        with d.Else():
                            hidden_few()
                    assert made == per_job, made
                    def results_ready():
                        d.wait_ge(cur_ready, j + 1)
                        d.wait_ge(down_done, 2 * j + 2)
                    with d.If(n > P):
                        with d.If(n > P + FEW):
                            results_ready()
                            V.tensor_scalar(y[:, 1, 512:], py[1][1][:, :], gate_cur[:, 1:2], None, ALU.mult)
                        with d.Else():
                            results_ready()
                            V.tensor_scalar(y[0:FEW, 1, 512:], py[1][1][FEW:P, :], gate_cur[FEW:P, 1:2], None, ALU.mult)
                    with d.Else():
                        d.nop()
                    with d.If(n > FEW):
                        results_ready()
                        V.tensor_scalar(y[:, 0, 512:], py[0][1][:, :], gate_cur[:, 0:1], None, ALU.mult
                                        ).then_inc(y_read[1], 1)
                    with d.Else():
                        results_ready()
                        V.tensor_scalar(y[0:FEW, 0, 512:], py[0][1][FEW:P, :], gate_cur[FEW:P, 0:1], None, ALU.mult
                                        ).then_inc(y_read[1], 1)
                with d.Else():
                    d.nop()
            fc = Chain(d, sem("ln2_chain"))
            d.wait_ge(ln2_in, 32)

            def moments(i):
                m = rows(i)
                d.wait_ge(acc_in[i], 16)
                for h in range(2):
                    fc.mark(V.bn_stats(bn2[0:m, i % 2, h], fin[0:m, i, h * 512:(h + 1) * 512]))
                fc.wait()
                fc.do(V.bn_aggr(mv2[0:m, i, 0:2], bn2[0:m, i % 2].rearrange("p h s -> p (h s)")))
                V.tensor_scalar(mv2[0:m, i, 1:2], mv2[0:m, i, 1:2], EPS, None, ALU.add).then_inc(var2, 1)

            def shift(i):
                m = rows(i)
                d.wait_ge(rstd2, i + 1)
                fc.do(V.reciprocal(mv2[0:m, i, 2:3], mv2[0:m, i, 3:4]))
                V.scalar_tensor_tensor(mv2[0:m, i, 4:5], mv2[0:m, i, 0:1], -1.0, mv2[0:m, i, 2:3], ALU.mult, ALU.mult
                                       ).then_inc(shift2, 1)

            def scale(i):
                m = rows(i)
                d.wait_ge(normed2, i + 1)
                V.tensor_tensor(fin[0:m, i], fin[0:m, i], l2g[0:m], ALU.mult).then_inc(scaled2, 1)

            for i in range(NT + 3):
                if i <= NT:
                    moments(i)
                if 1 <= i <= NT + 1:
                    shift(i - 1)
                if i >= 2:
                    scale(i - 2)


_OUTS = [(1, SEQ, D), (NS, 1, D), (1, 1, PBUF, POOLW), (1, 1, CBUF, CONVW), (1, 1, SEQ, NH, HD), (1, 1, SEQ, NH, HD),
         (1, NS, PBUF, POOLW), (1, NS, CBUF, CONVW), (1, NS, 1, NH, HD), (1, NS, 1, NH, HD)]


def lay_out(inputs):
    g = {k: np.asarray(a) for k, a in inputs.items()}

    def tiles(a, n):
        return np.ascontiguousarray(np.swapaxes(a.reshape(n, P, *a.shape[1:]), 0, 1))

    x = np.concatenate([g["x_prompt"][0], g["x_sample"][:, 0]], 0)
    blocks = np.zeros((P, 2, P), np.float32)
    for i in range(2 * 2):
        lo = (i % 2) * HD
        blocks[lo:lo + HD, i // 2, lo:lo + HD] = g["pool_w"][0, i]
    per_channel = [tiles(g["conv_w"][0].T, 3).reshape(P, -1)] + [
        tiles(g[k][0], n) for k, n in (("conv_b", 3), ("conv_ln_g", 3), ("conv_ln_b", 3), ("pool_scale", 2))]
    return {
        "xT": tiles(x.T, KT),
        "x_prompt": g["x_prompt"], "x_sample": g["x_sample"],
        "pool_prefix": tiles(np.transpose(g["state_pool"][0], (2, 0, 1)), 2),
        "conv_prefix": tiles(np.transpose(g["state_conv"][0], (2, 0, 1)), 3),
        "state_pool": g["state_pool"], "state_conv": g["state_conv"],
        "cache_k": g["cache_attn_k"].reshape(NS, PAST, ATTW), "cache_v": g["cache_attn_v"].reshape(NS, PAST, ATTW),
        "w_in": g["w_in"], "pool_w": blocks, "chan": np.concatenate(per_channel, 1), "w_o": g["w_o"],
        "ln1_g": g["ln1_g"][0], "ln1_b": g["ln1_b"][0],
        "router_w": tiles(g["router_w"][0], KT), "router_b": g["router_b"],
        "e_in": g["expert_w_in"][0],
        "e_bin": np.ascontiguousarray(np.transpose(g["expert_b_in"][0].reshape(NE, 2 * FT, P), (2, 0, 1))),
        "e_brow": g["expert_b_in"][0],
        "e_out": g["expert_w_out"][0], "e_bout": g["expert_b_out"],
        "ln2_g": g["ln2_g"][0], "ln2_b": g["ln2_b"][0],
        "consts": constants(), "ranks": slot_ranks(), "pbias": prompt_bias(),
    }


def kernel(**inputs):
    import concourse.bacc as bacc
    from concourse.bass_utils import run_bass_kernel_spmd

    nc = bacc.Bacc("TRN2", target_bir_lowering=False, num_devices=1)
    arrays, args = {}, []
    for name, a in lay_out(inputs).items():
        a = np.ascontiguousarray(a)
        arrays[f"in_{name}"] = a
        args.append(nc.dram_tensor(f"in_{name}", a.shape, mybir.dt.from_np(a.dtype), kind="ExternalInput").ap())
    for i, shape in enumerate(_OUTS):
        args.append(nc.dram_tensor(f"out_{i}", shape, F32, kind="ExternalOutput").ap())
    layer(nc, *args)
    r = run_bass_kernel_spmd(nc, [arrays], core_ids=[0])
    return tuple(r.results[0][f"out_{i}"] for i in range(len(_OUTS)))
```
